# Optimizing a Trainium2 kernel written in Bass

```python
import math
import jax
import jax.numpy as jnp
from jax import lax
import numpy as np

D_MODEL = 1024
BATCH = 1
SEQ = 1024
DEPTH = 2

GRID_W = 64
CTX_LEN = 256
Q_BLOCK = 128
EPS = 1e-6
ROPE_BASE = 10000.0
NEG_INF = -1e30

A_HEADS = 4
A_DQK = 64
A_DV = 2 * A_DQK
B_HEADS = 8
B_DH = 64
NA_WIN_H = 8
NA_WIN_W = 16
C_HEADS = 8
C_Q_LORA = 384
C_KV_LORA = 256
C_NOPE = 64
C_ROPE = 32
C_DV = 64
D_HEADS = 8
D_KV_HEADS = 2
D_DH = 64
D_WINDOW = 128
FFN_HIDDEN = 2816
CONV_W = 3

EVEN_SPLIT = (2 * A_HEADS * A_DQK, 2 * A_HEADS * A_DQK, A_HEADS * A_DV, B_HEADS * B_DH, B_HEADS * B_DH, B_HEADS * B_DH)
ODD_SPLIT = (C_Q_LORA, C_KV_LORA, C_ROPE, D_HEADS * D_DH, D_KV_HEADS * D_DH, D_KV_HEADS * D_DH)
EVEN_IN = sum(EVEN_SPLIT)
ODD_IN = sum(ODD_SPLIT)
EVEN_MIX = A_HEADS * A_DV + B_HEADS * B_DH
ODD_MIX = C_HEADS * C_DV + D_HEADS * D_DH
N_EVEN = (DEPTH + 1) // 2
N_ODD = DEPTH // 2

kernel_name = 'hybrid_diff_na_mla_swa_convffn_dit'

def rms_norm(x, g):
    xf = x.astype(jnp.float32)
    y = xf * lax.rsqrt(jnp.mean(xf * xf, axis=-1, keepdims=True) + EPS)
    return (y * g.astype(jnp.float32)).astype(x.dtype)

def modulate(h, shift, scale):
    return h * (1 + scale) + shift

def split_cols(p, sizes):
    return jnp.split(p, np.cumsum(sizes)[:-1].tolist(), axis=-1)

def axial_rope_tables(n_tokens, dim):
    t = jnp.arange(n_tokens, dtype=jnp.int32)
    row = (t // GRID_W).astype(jnp.float32)
    col = (t % GRID_W).astype(jnp.float32)
    quarter = dim // 4
    inv_freq = ROPE_BASE ** (-jnp.arange(quarter, dtype=jnp.float32) / quarter)
    ang = jnp.concatenate([row[:, None] * inv_freq, col[:, None] * inv_freq], axis=-1)
    return jnp.cos(ang), jnp.sin(ang)

def apply_rope(x, cos, sin):
    half = x.shape[-1] // 2
    x1, x2 = x[..., :half], x[..., half:]
    c = cos[None, :, None, :].astype(x.dtype)
    s = sin[None, :, None, :].astype(x.dtype)
    return jnp.concatenate([x1 * c - x2 * s, x1 * s + x2 * c], axis=-1)

def rope_tail(x, cos, sin):
    return jnp.concatenate([x[..., :C_NOPE], apply_rope(x[..., C_NOPE:], cos, sin)], axis=-1)

def sweep_query_blocks(fn, q):
    B, T = q.shape[:2]
    nb = T // Q_BLOCK
    qb = jnp.moveaxis(q.reshape((B, nb, Q_BLOCK) + q.shape[2:]), 1, 0)
    out = jnp.moveaxis(lax.map(fn, qb), 0, 1)
    return out.reshape((B, T) + out.shape[3:])

def softmax_attend(q, k, v, scale):
    s = jnp.einsum('bqhd,bkhd->bhqk', q, k, preferred_element_type=jnp.float32) * scale
    p = jax.nn.softmax(s, axis=-1).astype(v.dtype)
    return jnp.einsum('bhqk,bkhe->bqhe', p, v)

def diff_attend(q, k, v, lam, scale):
    s = jnp.einsum('bqhmd,bkhmd->bhmqk', q, k, preferred_element_type=jnp.float32) * scale
    p = jax.nn.softmax(s, axis=-1)
    w = p[:, :, 0] - lam * p[:, :, 1]
    return jnp.einsum('bhqk,bkhe->bqhe', w.astype(v.dtype), v)

def gqa_sink_attend(q, k, v, sink, scale, mask=None):
    s = jnp.einsum('bqhgd,bkhd->bhgqk', q, k, preferred_element_type=jnp.float32) * scale
    if mask is not None:
        s = jnp.where(mask, s, NEG_INF)
    Hk, G = q.shape[2], q.shape[3]
    sk = jnp.broadcast_to(sink.reshape(Hk, G)[None, :, :, None, None].astype(jnp.float32), s.shape[:-1] + (1,))
    p = jax.nn.softmax(jnp.concatenate([s, sk], axis=-1), axis=-1)[..., :-1]
    return jnp.einsum('bhgqk,bkhd->bqhgd', p.astype(v.dtype), v)

def neighbourhood_attend(q, k, v, k_ctx, v_ctx, rpb):
    B, T, H, dh = q.shape
    rows = T // GRID_W
    wh = min(NA_WIN_H, rows)
    ww = NA_WIN_W
    L = k_ctx.shape[1]
    scale = 1.0 / math.sqrt(dh)
    col_start = np.clip(np.arange(GRID_W) - ww // 2, 0, GRID_W - ww)
    col_idx = (col_start[:, None] + np.arange(ww)[None, :]).astype(np.int32)
    dc = (col_idx - np.arange(GRID_W)[:, None] + (NA_WIN_W - 1)).astype(np.int32)
    qg = q.reshape(B, rows, GRID_W, H, dh)
    kg = k.reshape(B, rows, GRID_W, H, dh)
    vg = v.reshape(B, rows, GRID_W, H, dh)

    def row_block(r):
        qr = lax.dynamic_index_in_dim(qg, r, axis=1, keepdims=False)
        rs = jnp.clip(r - wh // 2, 0, rows - wh)
        kn = lax.dynamic_slice_in_dim(kg, rs, wh, axis=1)[:, :, col_idx]
        vn = lax.dynamic_slice_in_dim(vg, rs, wh, axis=1)[:, :, col_idx]
        dr = rs + jnp.arange(wh) - r + (NA_WIN_H - 1)
        bias = jnp.transpose(rpb[:, dr[:, None, None], dc[None, :, :]], (0, 2, 1, 3))
        s_nb = jnp.einsum('bchd,brcwhd->bhcrw', qr, kn, preferred_element_type=jnp.float32) * scale + bias.astype(jnp.float32)
        s_ctx = jnp.einsum('bchd,blhd->bhcl', qr, k_ctx, preferred_element_type=jnp.float32) * scale
        p = jax.nn.softmax(jnp.concatenate([s_ctx, s_nb.reshape(B, H, GRID_W, wh * ww)], axis=-1), axis=-1).astype(v.dtype)
        p_ctx = p[..., :L]
        p_nb = p[..., L:].reshape(B, H, GRID_W, wh, ww)
        return jnp.einsum('bhcl,blhd->bchd', p_ctx, v_ctx) + jnp.einsum('bhcrw,brcwhd->bchd', p_nb, vn)

    out = lax.map(row_block, jnp.arange(rows))
    return jnp.moveaxis(out, 0, 1).reshape(B, T, H, dh)

def window_gqa_latent(q, k, v, k_ctx, v_ctx, sink):
    B, T = q.shape[:2]
    L = k_ctx.shape[1]
    span = Q_BLOCK + 2 * D_WINDOW
    scale = 1.0 / math.sqrt(D_DH)
    pad = ((0, 0), (D_WINDOW, D_WINDOW), (0, 0), (0, 0))
    kp = jnp.pad(k, pad)
    vp = jnp.pad(v, pad)
    ctx_ok = jnp.ones((Q_BLOCK, L), dtype=bool)

    def band_block(b):
        start = b * Q_BLOCK
        qi = lax.dynamic_slice_in_dim(q, start, Q_BLOCK, axis=1)
        ki = lax.dynamic_slice_in_dim(kp, start, span, axis=1)
        vi = lax.dynamic_slice_in_dim(vp, start, span, axis=1)
        qpos = start + jnp.arange(Q_BLOCK)
        kpos = start - D_WINDOW + jnp.arange(span)
        band = (jnp.abs(kpos[None, :] - qpos[:, None]) <= D_WINDOW) & (kpos >= 0)[None, :] & (kpos < T)[None, :]
        mask = jnp.concatenate([ctx_ok, band], axis=-1)
        return gqa_sink_attend(qi, jnp.concatenate([k_ctx, ki], axis=1), jnp.concatenate([v_ctx, vi], axis=1), sink, scale, mask)

    out = lax.map(band_block, jnp.arange(T // Q_BLOCK))
    return jnp.moveaxis(out, 0, 1).reshape(B, T, D_HEADS * D_DH)

def even_mixer(h, hc, w_in, w_out, a_q_norm, a_k_norm, a_lam_q1, a_lam_k1, a_lam_q2, a_lam_k2, a_subln,
               b_q_norm, b_k_norm, b_rpb, lam_init, with_ctx):
    B, T, _ = h.shape
    cos, sin = axial_rope_tables(T, A_DQK)
    scale_a = 1.0 / math.sqrt(A_DQK)

    def project(hh, use_rope, need_q):
        Bh, Th, _ = hh.shape
        qa, ka, va, qb, kb, vb = split_cols(hh @ w_in, EVEN_SPLIT)
        ka = rms_norm(ka.reshape(Bh, Th, 2 * A_HEADS, A_DQK), a_k_norm)
        kb = rms_norm(kb.reshape(Bh, Th, B_HEADS, B_DH), b_k_norm)
        if use_rope:
            ka = apply_rope(ka, cos, sin)
        ka = ka.reshape(Bh, Th, A_HEADS, 2, A_DQK)
        va = va.reshape(Bh, Th, A_HEADS, A_DV)
        vb = vb.reshape(Bh, Th, B_HEADS, B_DH)
        if need_q:
            qa = rms_norm(qa.reshape(Bh, Th, 2 * A_HEADS, A_DQK), a_q_norm)
            if use_rope:
                qa = apply_rope(qa, cos, sin)
            qa = qa.reshape(Bh, Th, A_HEADS, 2, A_DQK)
            qb = rms_norm(qb.reshape(Bh, Th, B_HEADS, B_DH), b_q_norm)
        else:
            qa = qb = None
        return qa, ka, va, qb, kb, vb

    lam = (jnp.exp(jnp.sum(a_lam_q1 * a_lam_k1).astype(jnp.float32))
           - jnp.exp(jnp.sum(a_lam_q2 * a_lam_k2).astype(jnp.float32)) + lam_init)
    qa, ka, va, qb, kb, vb = project(h, True, True)
    qa_c, ka_c, va_c, qb_c, kb_c, vb_c = project(hc, False, with_ctx)

    def merge(oa, ob):
        Bo, To = oa.shape[:2]
        oa = rms_norm(oa, a_subln) * (1.0 - lam_init)
        return jnp.concatenate([oa.reshape(Bo, To, -1), ob.reshape(Bo, To, -1)], axis=-1) @ w_out

    ka_all = jnp.concatenate([ka_c, ka], axis=1)
    va_all = jnp.concatenate([va_c, va], axis=1)
    oa = sweep_query_blocks(lambda qi: diff_attend(qi, ka_all, va_all, lam, scale_a), qa)
    ob = neighbourhood_attend(qb, kb, vb, kb_c, vb_c, b_rpb)
    y = merge(oa, ob)
    yc = None
    if with_ctx:
        yc = merge(diff_attend(qa_c, ka_c, va_c, lam, scale_a), softmax_attend(qb_c, kb_c, vb_c, 1.0 / math.sqrt(B_DH)))
    return y, yc

def odd_mixer(h, hc, w_in, w_out, c_q_a_norm, c_w_qb, c_kv_a_norm, c_w_kvb, c_q_norm, c_k_norm,
              d_q_norm, d_k_norm, d_sink, with_ctx):
    B, T, _ = h.shape
    cos_c, sin_c = axial_rope_tables(T, C_ROPE)
    cos_d, sin_d = axial_rope_tables(T, D_DH)
    scale_c = 1.0 / math.sqrt(C_NOPE + C_ROPE)

    def project(hh, use_rope, need_q):
        Bh, Th, _ = hh.shape
        cq, ckv, ckr, dq, dk, dv = split_cols(hh @ w_in, ODD_SPLIT)
        kv = (rms_norm(ckv, c_kv_a_norm) @ c_w_kvb).reshape(Bh, Th, C_HEADS, C_NOPE + C_DV)
        mk = jnp.concatenate([kv[..., :C_NOPE], jnp.broadcast_to(ckr[:, :, None, :], (Bh, Th, C_HEADS, C_ROPE))], axis=-1)
        mk = rms_norm(mk, c_k_norm)
        mv = kv[..., C_NOPE:]
        gk = rms_norm(dk.reshape(Bh, Th, D_KV_HEADS, D_DH), d_k_norm)
        gv = dv.reshape(Bh, Th, D_KV_HEADS, D_DH)
        if use_rope:
            mk = rope_tail(mk, cos_c, sin_c)
            gk = apply_rope(gk, cos_d, sin_d)
        mq = gq = None
        if need_q:
            mq = (rms_norm(cq, c_q_a_norm) @ c_w_qb).reshape(Bh, Th, C_HEADS, C_NOPE + C_ROPE)
            mq = rms_norm(mq, c_q_norm)
            gq = rms_norm(dq.reshape(Bh, Th, D_HEADS, D_DH), d_q_norm)
            if use_rope:
                mq = rope_tail(mq, cos_c, sin_c)
                gq = apply_rope(gq, cos_d, sin_d)
            gq = gq.reshape(Bh, Th, D_KV_HEADS, D_HEADS // D_KV_HEADS, D_DH)
        return mq, mk, mv, gq, gk, gv

    mq, mk, mv, gq, gk, gv = project(h, True, True)
    mq_c, mk_c, mv_c, gq_c, gk_c, gv_c = project(hc, False, with_ctx)

    mk_all = jnp.concatenate([mk_c, mk], axis=1)
    mv_all = jnp.concatenate([mv_c, mv], axis=1)
    om = sweep_query_blocks(lambda qi: softmax_attend(qi, mk_all, mv_all, scale_c), mq)
    og = window_gqa_latent(gq, gk, gv, gk_c, gv_c, d_sink)
    y = jnp.concatenate([om.reshape(B, T, -1), og], axis=-1) @ w_out
    yc = None
    if with_ctx:
        L = hc.shape[1]
        om_c = softmax_attend(mq_c, mk_c, mv_c, scale_c).reshape(B, L, -1)
        og_c = gqa_sink_attend(gq_c, gk_c, gv_c, d_sink, 1.0 / math.sqrt(D_DH)).reshape(B, L, -1)
        yc = jnp.concatenate([om_c, og_c], axis=-1) @ w_out
    return y, yc

def conv_ffn(h, w_up, conv_w, conv_b, w_down):
    T = h.shape[1]
    u = h @ w_up
    half = CONV_W // 2
    up = jnp.pad(u, ((0, 0), (half, half), (0, 0)))
    u = conv_b + up[:, 0:T] * conv_w[0]
    for j in range(1, CONV_W):
        u = u + up[:, j:j + T] * conv_w[j]
    a, g = jnp.split(u, 2, axis=-1)
    return (a * jax.nn.silu(g)) @ w_down

def setup_inputs(seed: int = 0) -> dict:
    key = jax.random.key(seed)
    ks = list(jax.random.split(key, 40))

    def nrm(shape, s):
        return s * jax.random.normal(ks.pop(), shape, jnp.float32)

    def gain(shape):
        return 1.0 + nrm(shape, 0.05)

    D, F = D_MODEL, FFN_HIDDEN
    return {
        'x': nrm((BATCH, SEQ, D), 1.0),
        'c': nrm((BATCH, D), 1.0),
        'ctx': nrm((BATCH, CTX_LEN, D), 1.0),
        'c_ctx': nrm((D,), 1.0),
        'ada_w': nrm((DEPTH, D, 6 * D), 0.5 * D ** -0.5),
        'ada_b': nrm((DEPTH, 6 * D), 0.01),
        'norm_mix': gain((DEPTH, D)),
        'norm_ffn': gain((DEPTH, D)),
        'ffn_up': nrm((DEPTH, D, 2 * F), D ** -0.5),
        'ffn_conv_w': nrm((DEPTH, CONV_W, 2 * F), CONV_W ** -0.5),
        'ffn_conv_b': nrm((DEPTH, 2 * F), 0.01),
        'ffn_down': nrm((DEPTH, F, D), F ** -0.5),
        'ev_w_in': nrm((N_EVEN, D, EVEN_IN), D ** -0.5),
        'ev_w_out': nrm((N_EVEN, EVEN_MIX, D), EVEN_MIX ** -0.5),
        'a_q_norm': gain((N_EVEN, A_DQK)),
        'a_k_norm': gain((N_EVEN, A_DQK)),
        'a_lam_q1': nrm((N_EVEN, A_DQK), 0.1),
        'a_lam_k1': nrm((N_EVEN, A_DQK), 0.1),
        'a_lam_q2': nrm((N_EVEN, A_DQK), 0.1),
        'a_lam_k2': nrm((N_EVEN, A_DQK), 0.1),
        'a_subln': gain((N_EVEN, A_DV)),
        'b_q_norm': gain((N_EVEN, B_DH)),
        'b_k_norm': gain((N_EVEN, B_DH)),
        'b_rpb': nrm((N_EVEN, B_HEADS, 2 * NA_WIN_H - 1, 2 * NA_WIN_W - 1), 0.1),
        'od_w_in': nrm((N_ODD, D, ODD_IN), D ** -0.5),
        'od_w_out': nrm((N_ODD, ODD_MIX, D), ODD_MIX ** -0.5),
        'c_q_a_norm': gain((N_ODD, C_Q_LORA)),
        'c_w_qb': nrm((N_ODD, C_Q_LORA, C_HEADS * (C_NOPE + C_ROPE)), C_Q_LORA ** -0.5),
        'c_kv_a_norm': gain((N_ODD, C_KV_LORA)),
        'c_w_kvb': nrm((N_ODD, C_KV_LORA, C_HEADS * (C_NOPE + C_DV)), C_KV_LORA ** -0.5),
        'c_q_norm': gain((N_ODD, C_NOPE + C_ROPE)),
        'c_k_norm': gain((N_ODD, C_NOPE + C_ROPE)),
        'd_q_norm': gain((N_ODD, D_DH)),
        'd_k_norm': gain((N_ODD, D_DH)),
        'd_sink': nrm((N_ODD, D_HEADS), 0.5),
    }

def reference(x, c, ctx, c_ctx, ada_w, ada_b, norm_mix, norm_ffn, ffn_up, ffn_conv_w, ffn_conv_b, ffn_down,
              ev_w_in, ev_w_out, a_q_norm, a_k_norm, a_lam_q1, a_lam_k1, a_lam_q2, a_lam_k2, a_subln,
              b_q_norm, b_k_norm, b_rpb, od_w_in, od_w_out, c_q_a_norm, c_w_qb, c_kv_a_norm, c_w_kvb,
              c_q_norm, c_k_norm, d_q_norm, d_k_norm, d_sink):
    xc = ctx
    for l in range(DEPTH):
        last = l == DEPTH - 1
        mod = (jax.nn.silu(c) @ ada_w[l] + ada_b[l])[:, None, :]
        modc = (jax.nn.silu(c_ctx) @ ada_w[l] + ada_b[l])[None, None, :]
        sh1, sc1, g1, sh2, sc2, g2 = jnp.split(mod, 6, axis=-1)
        csh1, csc1, cg1, csh2, csc2, cg2 = jnp.split(modc, 6, axis=-1)
        h = modulate(rms_norm(x, norm_mix[l]), sh1, sc1)
        hc = modulate(rms_norm(xc, norm_mix[l]), csh1, csc1)
        i = l // 2
        if l % 2 == 0:
            lam_init = 0.8 - 0.6 * math.exp(-0.3 * l)
            y, yc = even_mixer(h, hc, ev_w_in[i], ev_w_out[i], a_q_norm[i], a_k_norm[i], a_lam_q1[i], a_lam_k1[i],
                               a_lam_q2[i], a_lam_k2[i], a_subln[i], b_q_norm[i], b_k_norm[i], b_rpb[i],
                               lam_init, not last)
        else:
            y, yc = odd_mixer(h, hc, od_w_in[i], od_w_out[i], c_q_a_norm[i], c_w_qb[i], c_kv_a_norm[i], c_w_kvb[i],
                              c_q_norm[i], c_k_norm[i], d_q_norm[i], d_k_norm[i], d_sink[i], not last)
        x = x + g1 * y
        x = x + g2 * conv_ffn(modulate(rms_norm(x, norm_ffn[l]), sh2, sc2), ffn_up[l], ffn_conv_w[l], ffn_conv_b[l], ffn_down[l])
        if not last:
            xc = xc + cg1 * yc
            xc = xc + cg2 * conv_ffn(modulate(rms_norm(xc, norm_ffn[l]), csh2, csc2), ffn_up[l], ffn_conv_w[l], ffn_conv_b[l], ffn_down[l])
    return x


_drawn_inputs = setup_inputs


def setup_inputs(seed=0):
    import zlib

    import numpy as np

    out = dict(_drawn_inputs(seed))
    spreads = {}
    factors = {'ada_b': 3.758,
     'norm_mix': 8.0,
     'norm_ffn': 2.679,
     'ffn_conv_b': 8.0,
     'a_q_norm': 8.0,
     'a_k_norm': 8.0,
     'a_lam_q1': 64.0,
     'a_lam_k1': 8.0,
     'a_lam_q2': 64.0,
     'a_lam_k2': 64.0,
     'a_subln': 6.769,
     'b_q_norm': 8.0,
     'b_k_norm': 8.0,
     'b_rpb': 8.0,
     'c_q_a_norm': 8.0,
     'c_w_qb': 3.911,
     'c_kv_a_norm': 8.0,
     'c_q_norm': 8.0,
     'c_k_norm': 8.0,
     'd_q_norm': 8.0,
     'd_k_norm': 8.0,
     'd_sink': 8.0}
    for name, (base, spread) in spreads.items():
        noise = np.random.default_rng([zlib.crc32(name.encode()), seed]).standard_normal(out[name].shape)
        drawn = base * np.exp(spread * noise) if base else spread * noise
        out[name] = jnp.asarray(drawn.astype(out[name].dtype))
    for name, factor in factors.items():
        out[name] = (out[name] * factor).astype(out[name].dtype)
    return out
```

```python
import math
from contextlib import ExitStack

import concourse.bass as bass
import numpy as np
from concourse import mybir

F32 = mybir.dt.float32
F32R = mybir.dt.float32r
ACT = mybir.ActivationFunctionType
ALU = mybir.AluOpType
AX = mybir.AxisListType.X

P = 128
D = 1024
KD = D // P
LAT = 1024
CTX = 256
NT = CTX + LAT
DEPTH = 2
GRID_W = 64
EPS = 1e-6
NEG = -1e30
FFN = 2816
KF = FFN // P
NA_H, NA_W = 8, 16
HALF_ROWS = 2 * NA_H - 1
HALF_COLS = 2 * NA_W - 1
LAM_INIT = (0.8 - 0.6 * math.exp(0.0))
C_HEADS, C_DQK = 8, 96
Q_LORA, KV_LORA, C_ROPE = 384, 256, 32
ODD_CQ, ODD_CKV, ODD_CKR = 0, Q_LORA, Q_LORA + KV_LORA
ODD_DQ = ODD_CKR + C_ROPE
ODD_DK = ODD_DQ + 512
ODD_DV = ODD_DK + P
PRM_NORM_MIX, PRM_NORM_FFN, PRM_ADA_B = 0, DEPTH * KD, 2 * DEPTH * KD
PRM_CONV_W = PRM_ADA_B + DEPTH * 6 * KD
PRM_CONV_B = PRM_CONV_W + DEPTH * 3 * 2 * KF
PRM_N = PRM_CONV_B + DEPTH * 2 * KF
GV_AQ, GV_AK, GV_BQ, GV_BK, GV_DQ, GV_DK, GV_CQ, GV_CK, GV_SUB, GV_CQA, GV_CKVA = 0, 1, 2, 3, 4, 5, 6, 7, 8, 9, 12
GV_N = 14
NA_KIND = [0, 1, 2, 2, 2, 2, 3, 4]
NA_D0 = [7, 5, 3, 3, 1]
NA_ROWS = [8, 8, 9, 8, 8]
NA_KEYS = 9 * GRID_W


def chunks(t0, t1, step=512):
    return [(a, min(a + step, t1)) for a in range(t0, t1, step)]


def sweep(eng, tiles, used):
    pairs = tiles // 2

    def one(it):
        return [(2 * it, 0, it + used[0], it, it + used[1]), (2 * it + 1, 1, it + used[1], it, it + used[0] + 1)]

    first = 1 if used[0] == 0 or pairs == 1 else 0
    if pairs and first:
        yield one(0)
    if pairs - first == 1:
        yield one(first)
    elif pairs - first > 1:
        with eng.Fori(first, pairs) as it:
            yield one(it)
    used[0] += pairs
    used[1] += pairs
    if tiles % 2:
        yield [(tiles - 1, 0, used[0], pairs, used[1])]
        used[0] += 1


class Stage:
    cleared = []

    def __init__(self, nc, name):
        self.nc, self.name, self.ctx, self.own = nc, name, ExitStack(), []

    def __enter__(self):
        return self

    def __exit__(self, *a):
        self.ctx.__exit__(*a)
        if self.own:
            for h in Stage.cleared:
                self.nc.release_semaphore(h)
            for h in self.own:
                self.nc.gpsimd.sem_clear(h)
            Stage.cleared = self.own

    def sb(self, name, shape, dt=F32):
        return self.ctx.enter_context(self.nc.sbuf_tensor(f"{self.name}_{name}", shape, dt))

    def ps(self, name, shape, dt=F32):
        return self.ctx.enter_context(self.nc.psum_tensor(f"{self.name}_{name}", shape, dt))

    def sem(self, name):
        self.own.append(self.nc.alloc_semaphore(f"{self.name}_{name}"))
        return self.own[-1]

    def sems(self, name, n=2):
        return [self.sem(f"{name}{i}") for i in range(n)]

    def block(self):
        return self.ctx.enter_context(self.nc.Block())


def load_parameters(nc, G, IN):
    with Stage(nc, "par") as st:
        rows = st.sb("rows", [P, 5, P])
        vec = st.sb("vec", [16, P])
        svec = st.sb("svec", [16, P])
        lamv = st.sb("lamv", [64, 4])
        prod = st.sb("prod", [64, 2])
        lexp = st.sb("lexp", [P, 2])
        sink_row = st.sb("sink_row", [1, 8])
        tps = st.ps("tps", [P, 4, P])
        vps = st.ps("vps", [P, 512])
        consts, loaded = st.sem("consts"), st.sem("loaded")
        cleared = st.sem("cleared")
        silu, turned, turned_v, copied = st.sem("silu"), st.sem("turned"), st.sem("turned_v"), st.sem("copied")
        lam_prod, lam_sum, lam_exp, lam_diff = st.sem("lam_prod"), st.sem("lam_sum"), st.sem("lam_exp"), st.sem("lam_diff")
        done = st.sem("done")
        fill = st.sb("fill", [P, 8 * HALF_ROWS * GRID_W * GRID_W // P])
        filled, padded, rpb_in = st.sem("filled"), st.sem("padded"), st.sem("rpb_in")
        block = st.block()
        nconv = DEPTH * 3 * 2 * KF
        conv_w = IN["ffn_conv_w"].rearrange("l j (t p) -> (l j t) p", p=P)
        conv_b = IN["ffn_conv_b"].rearrange("l (t p) -> (l t) p", p=P)
        small = [("a_q_norm", GV_AQ), ("a_k_norm", GV_AK), ("b_q_norm", GV_BQ), ("b_k_norm", GV_BK),
                 ("d_q_norm", GV_DQ), ("d_k_norm", GV_DK)]
        loads = []
        for n, c in small:
            for half in (0, 64):
                loads.append((G.GV[half:half + 64, c:c + 1], IN[n].rearrange("a d -> d a")))
        for n, c in (("c_q_norm", GV_CQ), ("c_k_norm", GV_CK)):
            loads.append((G.GV[0:C_DQK, c:c + 1], IN[n].rearrange("a d -> d a")))
        loads.append((G.GV[:, GV_SUB:GV_SUB + 1], IN["a_subln"].rearrange("a d -> d a")))
        for n, c, w in (("c_q_a_norm", GV_CQA, Q_LORA), ("c_kv_a_norm", GV_CKVA, KV_LORA)):
            for k in range(w // P):
                loads.append((G.GV[:, c + k:c + k + 1], IN[n][:, k * P:(k + 1) * P].rearrange("a d -> d a")))
        for i, n in enumerate(("a_lam_q1", "a_lam_k1", "a_lam_q2", "a_lam_k2")):
            loads.append((lamv[:, i:i + 1], IN[n].rearrange("a d -> d a")))
        loads.append((sink_row[:, :], IN["d_sink"]))
        loads.append((vec[0:8, :], IN["c"].rearrange("a (k p) -> (a k) p", p=P)))
        loads.append((vec[8:16, :], IN["c_ctx"].rearrange("(k p) -> k p", p=P)))
        loads.append((rows[0:16, 0, :], IN["norm_mix"].rearrange("l (k p) -> (l k) p", p=P)))
        loads.append((rows[16:32, 0, :], IN["norm_ffn"].rearrange("l (k p) -> (l k) p", p=P)))
        loads.append((rows[32:128, 0, :], IN["ada_b"].rearrange("l (k p) -> (l k) p", p=P)))
        loads.append((rows[:, 1, :], conv_w[0:128]))
        loads.append((rows[:, 2, :], conv_w[128:256]))
        loads.append((rows[0:8, 3, :], conv_w[256:nconv]))
        loads.append((rows[8:96, 3, :], conv_b))
        assert nconv == 264 and PRM_CONV_W == P

        @block.sync
        def _(sp):
            sp.dma_start(G.IDENT[:, :], IN["k_ident"]).then_inc(consts, 16)
            sp.dma_start(G.BLK64[:, :], IN["k_blk64"]).then_inc(consts, 16)
            sp.dma_start(G.ROT[:, :], IN["k_rot"]).then_inc(consts, 16)
            sp.dma_start(G.ROT96[:, :], IN["k_rot96"]).then_inc(consts, 16)
            sp.wait_ge(cleared, 1)
            for dst, src in loads:
                sp.dma_start(dst, src).then_inc(loaded, 16)
            sp.wait_ge(filled, 1)
            sp.dma_start(G.RPB.rearrange("h r c k -> (h r c k)").rearrange("(p n) -> p n", p=P), fill[:, :]).then_inc(padded, 16)
            sp.wait_ge(padded, 16)
            edge = NA_W // 2
            for h in range(8):
                dst = bass.AP(tensor=G.RPB.tensor, offset=h * HALF_ROWS * GRID_W * GRID_W + edge * GRID_W,
                              ap=[[GRID_W * GRID_W, HALF_ROWS], [GRID_W + 1, GRID_W - NA_W + 1], [1, NA_W]])
                src = bass.AP(tensor=IN["b_rpb"].tensor, offset=h * HALF_ROWS * HALF_COLS + NA_W - 1 - edge,
                              ap=[[HALF_COLS, HALF_ROWS], [0, GRID_W - NA_W + 1], [1, NA_W]])
                sp.dma_start(dst, src).then_inc(rpb_in, 16)
            edges = list(range(edge)) + list(range(GRID_W - edge + 1, GRID_W))
            for c in edges:
                k0 = 0 if c < edge else GRID_W - NA_W
                sp.dma_start(G.RPB[:, :, c, k0:k0 + NA_W],
                             IN["b_rpb"][0, :, :, k0 - c + NA_W - 1:k0 - c + 2 * NA_W - 1]).then_inc(rpb_in, 16)
            sp.wait_ge(rpb_in, 16 * (8 + len(edges)))

        @block.gpsimd
        def _(pool):
            pool.memset(G.GV[:, :], 0.0).then_inc(cleared, 1)
            pool.memset(G.ONES[:, :], 1.0).then_inc(done, 1)
            pool.memset(G.EPSC[:, :], EPS).then_inc(done, 1)
            pool.memset(fill[:, :], NEG).then_inc(filled, 1)

        @block.scalar
        def _(act):
            act.wait_ge(loaded, 16 * len(loads))
            act.activation(svec[:, :], vec[:, :], ACT.Silu).then_inc(silu, 1)
            act.wait_ge(lam_sum, 2)
            act.activation(lexp[:, :], vps[:, 32:34], ACT.Exp).then_inc(lam_exp, 1)

        @block.tensor
        def _(pe):
            pe.wait_ge(consts, 64)
            pe.wait_ge(loaded, 16 * len(loads))
            for g in range(4):
                n = P if g < 3 else 96
                t = pe.transpose(tps[:, g, 0:n], rows[0:n, g, :], G.IDENT[0:n, 0:n])
            t.then_inc(turned, 1)
            pe.wait_ge(silu, 1)
            pe.transpose(vps[:, 0:16], svec[:, :], G.IDENT[0:16, 0:16]).then_inc(turned_v, 1)
            pe.wait_ge(done, 2)
            pe.wait_ge(lam_prod, 1)
            pe.matmul(vps[:, 32:34], G.ONES[0:64, :], prod[:, :], start=True, stop=True).then_inc(lam_sum, 1)
            pe.matmul(vps[:, 64:72], G.ONES[0:1, :], sink_row[:, :], start=True, stop=True).then_inc(lam_sum, 1)

        @block.vector
        def _(dve):
            dve.wait_ge(loaded, 16 * len(loads))
            dve.wait_ge(consts, 64)
            dve.tensor_tensor(prod[:, :], lamv[:, 0:4:2], lamv[:, 1:4:2], ALU.mult).then_inc(lam_prod, 1)
            qcols = [GV_AQ, GV_BQ, GV_DQ]
            for i, c in enumerate(qcols):
                dve.tensor_scalar(G.GV[:, c:c + 1], G.GV[:, c:c + 1], 64 ** -0.5, None, ALU.mult).then_inc(copied, 1)
            dve.tensor_scalar(G.GV[:, GV_CQ:GV_CQ + 1], G.GV[:, GV_CQ:GV_CQ + 1], C_DQK ** -0.5, None,
                              ALU.mult).then_inc(copied, 1)
            dve.tensor_scalar(G.GV[:, GV_SUB:GV_SUB + 1], G.GV[:, GV_SUB:GV_SUB + 1], 1.0 - LAM_INIT, None,
                              ALU.mult).then_inc(copied, 1)
            dve.wait_ge(copied, 5)
            for i, c in enumerate((GV_AQ, GV_AK, GV_DQ, GV_DK)):
                dve.tensor_scalar(G.ROTG[:, i, :], G.ROT[:, :], G.GV[:, c:c + 1], None, ALU.mult).then_inc(copied, 1)
            for i, c in enumerate((GV_CQ, GV_CK)):
                dve.tensor_scalar(G.ROTG[0:C_DQK, 4 + i, 0:C_DQK], G.ROT96[:, :], G.GV[0:C_DQK, c:c + 1], None,
                                  ALU.mult).then_inc(copied, 1)
            dve.wait_ge(turned, 1)
            dve.tensor_copy(G.PRM[:, 0:384], tps[:, 0:3, :].rearrange("p a b -> p (a b)")).then_inc(copied, 1)
            dve.tensor_copy(G.PRM[:, 384:PRM_N], tps[:, 3, 0:96]).then_inc(copied, 1)
            dve.wait_ge(turned_v, 1)
            dve.wait_ge(lam_sum, 2)
            dve.wait_ge(lam_exp, 1)
            dve.tensor_copy(G.CVEC[:, :], vps[:, 0:16]).then_inc(copied, 1)
            dve.tensor_copy(G.SINK[:, :], vps[:, 64:72]).then_inc(copied, 1)
            dve.tensor_tensor(G.NLAM[:, :], lexp[:, 1:2], lexp[:, 0:1], ALU.subtract).then_inc(lam_diff, 1)
            dve.wait_ge(lam_diff, 1)
            dve.tensor_scalar(G.NLAM[:, :], G.NLAM[:, :], -LAM_INIT, None, ALU.add).then_inc(lam_diff, 1)
            dve.wait_ge(lam_diff, 2)
            dve.tensor_scalar(G.LINV[:, :], G.NLAM[:, :], -1.0, 1.0, ALU.mult, ALU.max).then_inc(lam_diff, 1)
            dve.wait_ge(lam_diff, 3)
            dve.tensor_tensor(G.LINV[:, :], G.LINV[:, :], G.NLAM[:, :], ALU.max).then_inc(lam_diff, 1)
            dve.wait_ge(lam_diff, 4)
            dve.reciprocal(G.LINV[:, :], G.LINV[:, :]).then_inc(lam_diff, 1)
            dve.wait_ge(lam_diff, 5)
            dve.tensor_tensor(G.NLAM[:, :], G.NLAM[:, :], G.LINV[:, :], ALU.mult).then_inc(copied, 1)
            dve.tensor_scalar(G.EPSL[:, :], G.LINV[:, :], G.LINV[:, 0:1], EPS, ALU.mult, ALU.mult).then_inc(copied, 1)


def transpose_in(nc, G, IN):
    with Stage(nc, "xin") as st:
        tok = st.sb("tok", [P, 2, D])
        xt = st.sb("xt", [P, 2, KD, P])
        tps = st.ps("tps", [P, 2, KD, P])
        load, turn, copy_a, copy_v, store = (st.sems(n) for n in ("load", "turn", "copy_a", "copy_v", "store"))
        block = st.block()
        X = IN["x"].rearrange("a (t p) d -> (a t) p d", p=P)
        C = IN["ctx"].rearrange("a (t p) d -> (a t) p d", p=P)
        XT = G.X.rearrange("(k p) t -> p k t", p=P)
        jobs = [(C, CTX // P, 0), (X, LAT // P, CTX)]

        @block.sync
        def _(sp):
            used = [0, 0]
            for src, n, t0 in jobs:
                for its in sweep(sp, n, used):
                    for m, s, u, it, other in its:
                        sp.wait_ge(turn[s], u)
                        sp.dma_start(tok[:, s, :], src[bass.ds(m, 1)].rearrange("a p d -> (a p) d")).then_inc(load[s], 16)

        @block.tensor
        def _(pe):
            used = [0, 0]
            for src, n, t0 in jobs:
                for its in sweep(pe, n, used):
                    for m, s, u, it, other in its:
                        pe.wait_ge(load[s], 16 * u + 16)
                        pe.wait_ge(copy_a[s], u)
                        pe.wait_ge(copy_v[s], u)
                        for k in range(KD):
                            t = pe.transpose(tps[:, s, k, :], tok[:, s, k * P:(k + 1) * P], G.IDENT[:, :])
                        t.then_inc(turn[s], 1)

        @block.scalar
        def _(act):
            used = [0, 0]
            for src, n, t0 in jobs:
                for its in sweep(act, n, used):
                    for m, s, u, it, other in its:
                        act.wait_ge(turn[s], u + 1)
                        act.wait_ge(store[s], 16 * u)
                        act.activation(xt[:, s, 0:4, :], tps[:, s, 0:4, :], ACT.Copy).then_inc(copy_a[s], 1)
                        act.wait_ge(copy_a[s], u + 1)
                        act.wait_ge(copy_v[s], u + 1)
                        act.dma_start(XT[:, :, bass.ds(t0 + m * P, P)], xt[:, s, :, :]).then_inc(store[s], 16)
            for s in range(2):
                act.wait_ge(store[s], 16 * used[s])

        @block.vector
        def _(dve):
            used = [0, 0]
            for src, n, t0 in jobs:
                for its in sweep(dve, n, used):
                    for m, s, u, it, other in its:
                        dve.wait_ge(turn[s], u + 1)
                        dve.wait_ge(store[s], 16 * u)
                        dve.tensor_copy(xt[:, s, 4:8, :], tps[:, s, 4:8, :]).then_inc(copy_v[s], 1)


def modulation(nc, G, IN, layer):
    with Stage(nc, f"ada{layer}") as st:
        w = st.sb("w", [P, 2, KD, 512])
        row = st.sb("row", [2, 6 * D])
        mps = st.ps("mps", [2, 2, 512])
        cps = st.ps("cps", [P, 6 * KD * 2])
        load, mult, copy = (st.sems(n) for n in ("load", "mult", "copy"))
        turned, added, scaled = st.sem("turned"), st.sem("added"), st.sem("scaled")
        block = st.block()
        W = IN["ada_w"][layer].rearrange("(k p) n -> p k n", p=P)
        n = 6 * D // 512
        cvec = G.CVEC[:, :].rearrange("p (v k) -> p k v", v=2)

        @block.sync
        def _(sp):
            used = [0, 0]
            for its in sweep(sp, n, used):
                for m, s, u, it, other in its:
                    sp.wait_ge(mult[s], u)
                    sp.dma_start(w[:, s, :, :], W[:, :, bass.ds(m * 512, 512)]).then_inc(load[s], 16)

        @block.tensor
        def _(pe):
            used = [0, 0]
            for its in sweep(pe, n, used):
                for m, s, u, it, other in its:
                    pe.wait_ge(load[s], 16 * u + 16)
                    pe.wait_ge(copy[s], u)
                    for k in range(KD):
                        t = pe.matmul(mps[:, s, :], cvec[:, k, :], w[:, s, k, :], start=(k == 0), stop=(k == KD - 1))
                    t.then_inc(mult[s], 1)
            pe.wait_ge(copy[0], used[0])
            pe.wait_ge(copy[1], used[1])
            for j in range(6 * KD):
                t = pe.transpose(cps[:, 2 * j:2 * j + 2], row[:, j * P:(j + 1) * P], G.IDENT[0:2, 0:2])
            t.then_inc(turned, 1)

        @block.scalar
        def _(act):
            used = [0, 0]
            for its in sweep(act, n, used):
                for m, s, u, it, other in its:
                    act.wait_ge(mult[s], u + 1)
                    act.activation(row[:, bass.ds(m * 512, 512)], mps[:, s, :], ACT.Copy).then_inc(copy[s], 1)

        @block.vector
        def _(dve):
            dve.wait_ge(turned, 1)
            bias = G.PRM[:, PRM_ADA_B + layer * 48:PRM_ADA_B + layer * 48 + 48]
            mod = G.MOD[:, layer, :, :]
            cols = cps[:, :].rearrange("p (j v) -> p j v", v=2)
            for v in range(2):
                dve.tensor_tensor(mod[:, :, v], cols[:, :, v], bias, ALU.add).then_inc(added, 1)
            dve.wait_ge(added, 2)
            for which, norm, part in ((0, PRM_NORM_MIX, 1), (1, PRM_NORM_FFN, 4)):
                g = G.PRM[:, norm + layer * KD:norm + layer * KD + KD]
                for v in range(2):
                    dve.scalar_tensor_tensor(out=G.GS[:, layer, which, :, v], in0=mod[:, part * KD:part * KD + KD, v],
                                             scalar=1.0, in1=g, op0=ALU.add, op1=ALU.mult).then_inc(scaled, 1)


def operand(nc, G, name, src, kt, t0, t1, act_h, act_l, scale=None, shift=None, norm=True, mean_over=D, sub_tiles=0):
    T = t1 - t0
    with Stage(nc, name) as st:
        x = st.sb("x", [P, kt, T])
        sq = st.sb("sq", [P, 2, T])
        nr = kt if not norm else 1
        rs = st.sb("rs", [P, max(1, sub_tiles), T]) if not norm else st.sb("rs", [P, 1, T])
        ss = st.ps("ss", [P, 2, 1536])
        load = st.sems("load", kt)
        squared, summed, logged, rstd = (st.sem(n) for n in ("squared", "summed", "logged", "rstd"))
        normed, modded, hi, lo = (st.sem(n) for n in ("normed", "modded", "hi", "lo"))
        block = st.block()
        S = src.rearrange("(k p) t -> k p t", p=P)
        nsq = kt if norm else sub_tiles
        nrs = 1 if norm else sub_tiles
        cs = chunks(0, T)

        @block.sync
        def _(sp):
            for k in range(kt):
                sp.dma_start(x[:, k, :], S[k, :, t0:t1]).then_inc(load[k], 16)

        @block.tensor
        def _(pe):
            for k in range(nsq):
                pe.wait_ge(squared, k + 1)
                if not norm and k >= 2:
                    pe.wait_ge(logged, k - 1)
                for c, (a, b) in enumerate(cs):
                    t = pe.matmul(ss[:, 0 if norm else k % 2, a:b], G.ONES[:, :], sq[:, k % 2, a:b],
                                  start=(k == 0 or not norm), stop=(k == kt - 1 or not norm))
                t.then_inc(summed, 1)

        @block.scalar
        def _(act):
            def to_rstd(r):
                if not norm:
                    act.activation(rs[:, r, :], ss[:, r % 2, 0:T], ACT.Sqrt, scale=1.0 / mean_over,
                                   bias=G.EPSL[:, 0:1]).then_inc(logged, 1)
                    return
                act.activation(rs[:, r, :], ss[:, r % 2, 0:T], ACT.Ln, scale=1.0 / mean_over,
                               bias=G.EPSC[:, 0:1]).then_inc(logged, 1)
                act.wait_ge(logged, r + 1)
                act.activation(rs[:, r, :], rs[:, r, :], ACT.Exp, scale=-0.5).then_inc(rstd, 1)

            n_mod = 0
            for k in range(nsq):
                act.wait_ge(load[k], 16)
                if k >= 2:
                    act.wait_ge(summed, k - 1)
                act.activation(sq[:, k % 2, :], x[:, k, :], ACT.Square).then_inc(squared, 1)
                if not norm:
                    act.wait_ge(summed, k + 1)
                    to_rstd(k)
            if norm:
                act.wait_ge(summed, kt)
                to_rstd(0)
            for k in range(kt):
                if k < nsq or norm:
                    act.wait_ge(normed, k + 1)
                act.wait_ge(load[k], 16)
                if scale and scale(k):
                    for i, (sc, a, b) in enumerate(scale(k)):
                        if shift:
                            sh = shift(k)[i][0]
                            t = act.activation(x[:, k, a - t0:b - t0], x[:, k, a - t0:b - t0], ACT.Identity, scale=sc, bias=sh)
                        else:
                            t = act.activation(x[:, k, a - t0:b - t0], x[:, k, a - t0:b - t0], ACT.Identity, scale=sc)
                        t.then_inc(modded, 1)
                    n_mod += len(scale(k))
                    act.wait_ge(modded, n_mod)
                act.activation(act_h[:, k, 0:T], x[:, k, :], ACT.Copy).then_inc(hi, 1)

        @block.vector
        def _(dve):
            def finish(k):
                dve.wait_ge(hi, k + 1)
                dve.tensor_tensor(act_l[:, k, 0:T], x[:, k, :], act_h[:, k, 0:T].bitcast(F32), ALU.subtract).then_inc(lo, 1)
            for k in range(kt):
                if k < nsq or norm:
                    if not norm:
                        dve.wait_ge(logged, k + 1)
                        dve.reciprocal(rs[:, k, :], rs[:, k, :]).then_inc(rstd, 1)
                    dve.wait_ge(rstd, 1 if norm else k + 1)
                    dve.tensor_tensor(x[:, k, :], x[:, k, :], rs[:, 0 if norm else k, :], ALU.mult).then_inc(normed, 1)
                if k >= 1:
                    finish(k - 1)
            finish(kt - 1)


class Weights:

    def __init__(self, st, kt):
        self.kt = kt
        self.raw = st.sb("w_raw", [P, 2, kt, P])
        self.hi = st.sb("w_hi", [P, 2, kt, P], F32R)
        self.lo = st.sb("w_lo", [P, 2, kt, P], F32R)
        self.loaded, self.hi_ready, self.lo_ready = st.sems("w_loaded"), st.sems("w_hi_ready"), st.sems("w_lo_ready")
        self.multiplied = st.sems("multiplied")


def load_weights(sp, W, wd, segs):
    V = wd.rearrange("(k p) m -> p k m", p=P)
    used = [0, 0]
    for g in segs:
        for its in sweep(sp, g["tiles"], used):
            for m, s, u, it, other in its:
                sp.wait_ge(W.lo_ready[s], u)
                sp.dma_start(W.raw[:, s, :, 0:g["mw"]], V[:, :, bass.ds(g["col"](m, s, it), g["mw"])])\
                  .then_inc(W.loaded[s], 16)


def split_weights(pool, W, segs, ones):
    used = [0, 0]
    for g in segs:
        mw = g["mw"]
        for its in sweep(pool, g["tiles"], used):
            for m, s, u, it, other in its:
                pool.wait_ge(W.loaded[s], 16 * u + 16)
                pool.wait_ge(W.multiplied[s], u)
                pool.tensor_tensor(W.hi[:, s, :, 0:mw], W.raw[:, s, :, 0:mw],
                                   ones[:, 0:mw].unsqueeze(1).broadcast_to([P, W.kt, mw]), ALU.mult)\
                    .then_inc(W.hi_ready[s], 1)
                pool.wait_ge(W.hi_ready[s], u + 1)
                pool.tensor_tensor(W.lo[:, s, :, 0:mw], W.raw[:, s, :, 0:mw], W.hi[:, s, :, 0:mw].bitcast(F32),
                                   ALU.subtract).then_inc(W.lo_ready[s], 1)


def multiply(pe, W, act_h, act_l, acc, g, a0, s, u):
    mw = g["mw"]
    t0, t1 = g["toks"]
    pe.wait_ge(W.lo_ready[s], u + 1)
    for a, b in chunks(t0, t1):
        for k in range(W.kt):
            for w, x in ((W.hi, act_h), (W.hi, act_l), (W.lo, act_h)):
                t = pe.matmul(acc[0:mw, s, a - t0:b - t0], w[:, s, k, 0:mw], x[:, k, a - a0:b - a0],
                              start=(k == 0 and w is W.hi and x is act_h), stop=(k == W.kt - 1 and w is W.lo))
    t.then_inc(W.multiplied[s], 1)


def project_store(nc, G, name, wd, kt, act_h, act_l, a0, segs, out):
    with Stage(nc, name) as st:
        W = Weights(st, kt)
        ob = st.sb("ob", [P, 2, NT])
        acc = st.ps("acc", [P, 2, 1536])
        ev_a, ev_v, stored = (st.sems(n) for n in ("ev_a", "ev_v", "stored"))
        block = st.block()

        @block.sync
        def _(sp):
            load_weights(sp, W, wd, segs)

        @block.gpsimd
        def _(pool):
            split_weights(pool, W, segs, G.ONES)

        @block.tensor
        def _(pe):
            used = [0, 0]
            for g in segs:
                for its in sweep(pe, g["tiles"], used):
                    for m, s, u, it, other in its:
                        pe.wait_ge(ev_a[s], u)
                        pe.wait_ge(ev_v[s], u)
                        multiply(pe, W, act_h, act_l, acc, g, a0, s, u)

        @block.scalar
        def _(act):
            used = [0, 0]
            for g in segs:
                T, mw = g["toks"][1] - g["toks"][0], g["mw"]
                for its in sweep(act, g["tiles"], used):
                    for m, s, u, it, other in its:
                        act.wait_ge(W.multiplied[s], u + 1)
                        act.wait_ge(stored[s], 16 * u)
                        act.activation(ob[0:mw, s, 0:512], acc[0:mw, s, 0:512], ACT.Copy).then_inc(ev_a[s], 1)
                        act.wait_ge(ev_a[s], u + 1)
                        act.wait_ge(ev_v[s], u + 1)
                        act.dma_start(out[bass.ds(g["row"] + m * mw, mw), g["toks"][0]:g["toks"][1]],
                                      ob[0:mw, s, 0:T]).then_inc(stored[s], 16)
            for s in range(2):
                act.wait_ge(stored[s], 16 * used[s])

        @block.vector
        def _(dve):
            used = [0, 0]
            for g in segs:
                T, mw = g["toks"][1] - g["toks"][0], g["mw"]
                for its in sweep(dve, g["tiles"], used):
                    for m, s, u, it, other in its:
                        dve.wait_ge(W.multiplied[s], u + 1)
                        dve.wait_ge(stored[s], 16 * u)
                        dve.tensor_copy(ob[0:mw, s, 512:T], acc[0:mw, s, 512:T]).then_inc(ev_v[s], 1)


def project_heads(nc, G, name, wd, kt, act_h, act_l, a0, segs, out, tables=None, kr=None, v_out=None):
    with Stage(nc, name) as st:
        W = Weights(st, kt)
        cos, sin = st.sb("cos", [P, NT]), st.sb("sin", [P, NT])
        raw, sq, ob = st.sb("raw", [P, 2, NT]), st.sb("sq", [P, 2, NT]), st.sb("ob", [P, 2, NT])
        rs, rot = st.sb("rs", [P, NT]), st.sb("rot", [P, NT])
        vb = st.sb("vb", [P, 2, NT]) if v_out is not None else None
        acc, aux = st.ps("acc", [P, 2, 1536]), st.ps("aux", [P, 2, 512])
        tab, kr_in = st.sem("tab"), st.sem("kr_in")
        raw_ready, sq_ready, v_ready, normed, stored, v_stored = (
            st.sems(n) for n in ("raw_ready", "sq_ready", "v_ready", "normed", "stored", "v_stored"))
        aux_ready, aux_free = st.sems("aux_ready"), st.sems("aux_free")
        rstd, with_cos, with_rot = st.sem("rstd"), st.sem("with_cos"), st.sem("with_rot")
        block = st.block()

        def parts(g):
            T = g["toks"][1] - g["toks"][0]
            return chunks(0, T, T // 4 if T > 1024 else 512)

        def jobs(g):
            return len(parts(g)) * (2 if g["rope"] is not None else 1)

        def walk(eng, body):
            used, bank_uses, tiles, ropes = [0, 0], 0, 0, 0
            for g in segs:
                for its in sweep(eng, g["tiles"], used):
                    body(g, its, bank_uses, tiles, ropes)
                bank_uses += g["tiles"] * jobs(g) // 2
                tiles += g["tiles"]
                ropes += g["tiles"] if g["rope"] is not None else 0
            return used

        @block.sync
        def _(sp):
            if tables is not None:
                nr = tables[0].shape[0]
                sp.dma_start(cos[0:nr, :], tables[0]).then_inc(tab, 16)
                sp.dma_start(sin[0:nr, :], tables[1]).then_inc(tab, 16)
            if kr is not None:
                for s in range(2):
                    sp.dma_start(raw[64:C_DQK, s, :], kr).then_inc(kr_in, 16)
            load_weights(sp, W, wd, segs)

        @block.gpsimd
        def _(pool):
            split_weights(pool, W, segs, G.ONES)

        @block.tensor
        def _(pe):
            def body(g, its, bank_uses, tiles, ropes):
                rows, n = g["rows"], jobs(g)
                for m, s, u, it, other in its:
                    pe.wait_ge(raw_ready[s], u)
                    if v_out is not None:
                        pe.wait_ge(v_ready[s], u)
                    multiply(pe, W, act_h, act_l, acc, g, a0, s, u)
                for m, s, u, it, other in its:
                    pe.wait_ge(sq_ready[s], u + 1)
                    pe.wait_ge(raw_ready[s], u + 1)
                    work = [(g["ones"], sq, p) for p in parts(g)]
                    if g["rope"] is not None:
                        work += [(g["rope"], raw, p) for p in parts(g)]
                    for j, (mat, x, (a, b)) in enumerate(work):
                        pe.wait_ge(aux_free[j % 2], bank_uses + m * (n // 2) + j // 2)
                        pe.matmul(aux[0:rows, j % 2, 0:b - a], mat[0:rows, 0:rows], x[0:rows, s, a:b], start=True,
                                  stop=True).then_inc(aux_ready[j % 2], 1)
            walk(pe, body)

        @block.scalar
        def _(act):
            if kr is not None:
                act.wait_ge(kr_in, 32)

            def body(g, its, bank_uses, tiles, ropes):
                T, rows, own, n = g["toks"][1] - g["toks"][0], g["rows"], g["own"], jobs(g)
                for m, s, u, it, other in its:
                    act.wait_ge(W.multiplied[s], u + 1)
                    act.wait_ge(normed[s], u)
                    act.activation(raw[0:own, s, 0:T], acc[0:own, s, 0:T], ACT.Copy).then_inc(raw_ready[s], 1)
                    if v_out is not None:
                        act.wait_ge(v_stored[s], 16 * u)
                        act.activation(vb[64:P, s, 0:T], acc[64:P, s, 0:T], ACT.Copy).then_inc(v_ready[s], 1)
                    act.wait_ge(raw_ready[s], u + 1)
                    act.activation(sq[0:rows, s, 0:T], raw[0:rows, s, 0:T], ACT.Square).then_inc(sq_ready[s], 1)
                    if v_out is not None:
                        act.wait_ge(v_ready[s], u + 1)
                        act.dma_start(v_out[bass.ds(m * 64, 64), :], vb[64:P, s, 0:T]).then_inc(v_stored[s], 16)
                for m, s, u, it, other in its:
                    act.wait_ge(normed[s], u)
                    act.wait_ge(normed[1 - s], other)
                    for j, (a, b) in enumerate(parts(g)):
                        before = bank_uses + m * (n // 2) + j // 2
                        act.wait_ge(aux_ready[j % 2], before + 1)
                        act.activation(rs[0:rows, a:b], aux[0:rows, j % 2, 0:b - a], ACT.Ln, scale=1.0 / g["width"],
                                       bias=G.EPSC[0:rows, 0:1]).then_inc(aux_free[j % 2], 1)
                    for b in range(2):
                        act.wait_ge(aux_free[b], bank_uses + m * (n // 2) + len(parts(g)) // 2)
                    act.activation(rs[0:rows, 0:T], rs[0:rows, 0:T], ACT.Exp, scale=-0.5).then_inc(rstd, 1)
                for m, s, u, it, other in its:
                    act.wait_ge(normed[s], u + 1)
                    act.dma_start(out[bass.ds(g["row"] + m * rows, rows), g["toks"][0]:g["toks"][1]],
                                  ob[0:rows, s, 0:T]).then_inc(stored[s], 16)

            used = walk(act, body)
            for s in range(2):
                act.wait_ge(stored[s], 16 * used[s])
                if v_out is not None:
                    act.wait_ge(v_stored[s], 16 * used[s])

        @block.vector
        def _(dve):
            if tables is not None:
                dve.wait_ge(tab, 32)

            def body(g, its, bank_uses, tiles, ropes):
                (t0, t1), rows, n = g["toks"], g["rows"], jobs(g)
                T = t1 - t0
                gain = G.GV[0:rows, g["gain"]:g["gain"] + 1]
                for m, s, u, it, other in its:
                    dve.wait_ge(raw_ready[s], u + 1)
                    dve.wait_ge(stored[s], 16 * u)
                    x, o = raw[0:rows, s, 0:T], ob[0:rows, s, 0:T]
                    if g["rope"] is None:
                        dve.wait_ge(rstd, tiles + m + 1)
                        dve.scalar_tensor_tensor(out=o, in0=x, scalar=gain, in1=rs[0:rows, 0:T], op0=ALU.mult,
                                                 op1=ALU.mult).then_inc(normed[s], 1)
                        continue
                    dve.scalar_tensor_tensor(out=o, in0=x, scalar=gain, in1=cos[0:rows, t0:t1], op0=ALU.mult,
                                             op1=ALU.mult).then_inc(with_cos, 1)
                    ps = parts(g)
                    for i, (a, b) in enumerate(ps):
                        j = len(ps) + i
                        dve.wait_ge(aux_ready[j % 2], bank_uses + m * (n // 2) + j // 2 + 1)
                        dve.tensor_tensor(rot[0:rows, a:b], aux[0:rows, j % 2, 0:b - a], sin[0:rows, t0 + a:t0 + b],
                                          ALU.mult).then_inc(aux_free[j % 2], 1)
                    dve.wait_ge(with_cos, ropes + m + 1)
                    for b in range(2):
                        dve.wait_ge(aux_free[b], bank_uses + (m + 1) * (n // 2))
                    dve.tensor_tensor(o, o, rot[0:rows, 0:T], ALU.add).then_inc(with_rot, 1)
                    dve.wait_ge(with_rot, ropes + m + 1)
                    dve.wait_ge(rstd, tiles + m + 1)
                    dve.tensor_tensor(o, o, rs[0:rows, 0:T], ALU.mult).then_inc(normed[s], 1)
            walk(dve, body)


def project_residual(nc, G, name, wd, kt, act_h, act_l, a0, layer, toks, part):
    t0, t1 = toks
    T = t1 - t0
    segs = [dict(tiles=KD, mw=P, col=lambda m, s, it: m * P, toks=toks)]
    with Stage(nc, name) as st:
        W = Weights(st, kt)
        x = st.sb("x", [P, 2, T])
        acc = st.ps("acc", [P, 2, 1536])
        x_in, added, stored = (st.sems(n) for n in ("x_in", "added", "stored"))
        block = st.block()
        ranges = [(v, max(a, t0), b) for v, a, b in ((1, 0, CTX), (0, CTX, NT)) if b > t0]

        @block.sync
        def _(sp):
            load_weights(sp, W, wd, segs)

        @block.gpsimd
        def _(pool):
            split_weights(pool, W, segs, G.ONES)

        @block.tensor
        def _(pe):
            for its in sweep(pe, KD, [0, 0]):
                for m, s, u, it, other in its:
                    pe.wait_ge(added[s], len(ranges) * u)
                    multiply(pe, W, act_h, act_l, acc, segs[0], a0, s, u)

        @block.scalar
        def _(act):
            used = [0, 0]
            for its in sweep(act, KD, used):
                for m, s, u, it, other in its:
                    act.wait_ge(stored[s], 16 * u)
                    act.dma_start(x[:, s, :], G.X[bass.ds(m * P, P), t0:t1]).then_inc(x_in[s], 16)
                for m, s, u, it, other in its:
                    act.wait_ge(added[s], len(ranges) * (u + 1))
                    act.dma_start(G.X[bass.ds(m * P, P), t0:t1], x[:, s, :]).then_inc(stored[s], 16)
            for s in range(2):
                act.wait_ge(stored[s], 16 * used[s])

        @block.vector
        def _(dve):
            for its in sweep(dve, KD, [0, 0]):
                for m, s, u, it, other in its:
                    dve.wait_ge(x_in[s], 16 * u + 16)
                    dve.wait_ge(W.multiplied[s], u + 1)
                    for v, a, b in ranges:
                        gate = G.MOD[:, layer, bass.ds(part * KD + m, 1), v]
                        dve.scalar_tensor_tensor(out=x[:, s, a - t0:b - t0], in0=acc[:, s, a - t0:b - t0], scalar=gate,
                                                 in1=x[:, s, a - t0:b - t0], op0=ALU.mult, op1=ALU.add)\
                           .then_inc(added[s], 1)


def ffn_up(nc, G, name, wd, act_h, act_l, a0, layer, toks, out):
    t0, t1 = toks
    T = t1 - t0
    segs = [dict(tiles=2 * KF, mw=P, col=lambda m, s, it: (it + s * KF) * P, toks=toks)]
    seqs = [(max(a, t0) - t0, b - t0) for a, b in ((0, CTX), (CTX, NT)) if b > t0]
    nseq = len(seqs)
    with Stage(nc, name) as st:
        W = Weights(st, KD)
        u_ = st.sb("conv", [P, 2, T])
        sg = st.sb("sg", [P, T])
        acc = st.ps("acc", [P, 2, 1536])
        mid, left, right = st.sems("mid"), st.sems("left"), st.sems("right")
        silu, gated, stored = st.sem("silu"), st.sem("gated"), st.sem("stored")
        block = st.block()

        def tap(j, s, it):
            return G.PRM[:, bass.ds(PRM_CONV_W + (layer * 3 + j) * 2 * KF + s * KF + it, 1)]

        @block.sync
        def _(sp):
            load_weights(sp, W, wd, segs)

        @block.gpsimd
        def _(pool):
            split_weights(pool, W, segs, G.ONES)

        @block.tensor
        def _(pe):
            for its in sweep(pe, 2 * KF, [0, 0]):
                for m, s, u, it, other in its:
                    pe.wait_ge(mid[s], u)
                    pe.wait_ge(right[s], nseq * u)
                    multiply(pe, W, act_h, act_l, acc, segs[0], a0, s, u)

        @block.scalar
        def _(act):
            for its in sweep(act, 2 * KF, [0, 0]):
                for m, s, u, it, other in its:
                    act.wait_ge(W.multiplied[s], u + 1)
                    act.wait_ge(gated, u)
                    if s == 1:
                        act.wait_ge(silu, u)
                    bias = G.PRM[:, bass.ds(PRM_CONV_B + layer * 2 * KF + s * KF + it, 1)]
                    act.activation(u_[:, s, :], acc[:, s, 0:T], ACT.Identity, scale=tap(1, s, it), bias=bias)\
                       .then_inc(mid[s], 1)
                act.wait_ge(right[1], nseq * (its[1][2] + 1))
                act.activation(sg[:, :], u_[:, 1, :], ACT.Silu).then_inc(silu, 1)
                act.wait_ge(gated, its[1][2] + 1)
                act.dma_start(out[bass.ds(it * P, P), t0:t1], u_[:, 0, :]).then_inc(stored, 16)
                act.wait_ge(stored, 16 * (its[1][2] + 1))

        @block.vector
        def _(dve):
            for its in sweep(dve, 2 * KF, [0, 0]):
                for m, s, u, it, other in its:
                    dve.wait_ge(mid[s], u + 1)
                    for a, b in seqs:
                        dve.scalar_tensor_tensor(out=u_[:, s, a + 1:b], in0=acc[:, s, a:b - 1], scalar=tap(0, s, it),
                                                 in1=u_[:, s, a + 1:b], op0=ALU.mult, op1=ALU.add).then_inc(left[s], 1)
                    dve.wait_ge(left[s], nseq * (u + 1))
                    for a, b in seqs:
                        dve.scalar_tensor_tensor(out=u_[:, s, a:b - 1], in0=acc[:, s, a + 1:b], scalar=tap(2, s, it),
                                                 in1=u_[:, s, a:b - 1], op0=ALU.mult, op1=ALU.add).then_inc(right[s], 1)
                u = its[1][2]
                dve.wait_ge(silu, u + 1)
                dve.wait_ge(right[0], nseq * (u + 1))
                dve.tensor_tensor(u_[:, 0, :], u_[:, 0, :], sg[:, :], ALU.mult).then_inc(gated, 1)


def ffn_down(nc, G, name, wd, hid, layer, toks):
    t0, t1 = toks
    T = t1 - t0
    v = 1 if t1 <= CTX else 0
    with Stage(nc, name) as st:
        w_raw = st.sb("w_raw", [P, 2, D])
        w_hi, w_lo = st.sb("w_hi", [P, 2, D], F32R), st.sb("w_lo", [P, 2, D], F32R)
        h_raw = st.sb("h_raw", [P, 2, T])
        h_hi, h_lo = st.sb("h_hi", [P, 2, T], F32R), st.sb("h_lo", [P, 2, T], F32R)
        x = st.sb("x", [P, KD, T])
        acc = st.ps("acc", [P, KD, 512])
        w_in, h_in, w_hi_ready, w_lo_ready, h_hi_ready, h_lo_ready, multiplied = (
            st.sems(n) for n in ("w_in", "h_in", "w_hi_ready", "w_lo_ready", "h_hi_ready", "h_lo_ready", "multiplied"))
        w2_lo_ready = st.sems("w2_lo_ready")
        x_in, summed, added, stored = st.sem("x_in"), st.sem("summed"), st.sem("added"), st.sem("stored")
        block = st.block()
        X = G.X.rearrange("(k p) t -> p k t", p=P)

        @block.sync
        def _(sp):
            for its in sweep(sp, KF, [0, 0]):
                for k, s, u, it, other in its:
                    sp.wait_ge(w_lo_ready[s], u)
                    sp.wait_ge(w2_lo_ready[s], u)
                    sp.dma_start(w_raw[:, s, :], wd[bass.ds(k * P, P), :]).then_inc(w_in[s], 16)
                    sp.wait_ge(h_lo_ready[s], u)
                    sp.dma_start(h_raw[:, s, :], hid[bass.ds(k * P, P), t0:t1]).then_inc(h_in[s], 16)
            sp.dma_start(x[:, :, :], X[:, :, t0:t1]).then_inc(x_in, 16)
            for m in range(KD):
                sp.wait_ge(added, m + 1)
                sp.dma_start(X[:, m, t0:t1], x[:, m, :]).then_inc(stored, 16)
            sp.wait_ge(stored, 16 * KD)

        @block.gpsimd
        def _(pool):
            for its in sweep(pool, KF, [0, 0]):
                for k, s, u, it, other in its:
                    pool.wait_ge(w_in[s], 16 * u + 16)
                    pool.wait_ge(w_hi_ready[s], u + 1)
                    pool.wait_ge(multiplied[s], u)
                    pool.tensor_tensor(w_lo[:, s, 0:512], w_raw[:, s, 0:512], w_hi[:, s, 0:512].bitcast(F32),
                                       ALU.subtract).then_inc(w_lo_ready[s], 1)

        @block.scalar
        def _(act):
            for its in sweep(act, KF, [0, 0]):
                for k, s, u, it, other in its:
                    act.wait_ge(multiplied[s], u)
                    act.wait_ge(w_in[s], 16 * u + 16)
                    act.activation(w_hi[:, s, :], w_raw[:, s, :], ACT.Copy).then_inc(w_hi_ready[s], 1)
                    act.wait_ge(h_in[s], 16 * u + 16)
                    act.activation(h_hi[:, s, :], h_raw[:, s, :], ACT.Copy).then_inc(h_hi_ready[s], 1)

        @block.tensor
        def _(pe):
            def step(s, u, first, last):
                pe.wait_ge(w_lo_ready[s], u + 1)
                pe.wait_ge(w2_lo_ready[s], u + 1)
                pe.wait_ge(h_lo_ready[s], u + 1)
                for m in range(KD):
                    for w, h in ((w_hi, h_hi), (w_hi, h_lo), (w_lo, h_hi)):
                        t = pe.matmul(acc[:, m, 0:T], w[:, s, m * P:(m + 1) * P], h[:, s, :],
                                      start=first and w is w_hi and h is h_hi, stop=last and w is w_lo,
                                      skip_group_check=True)
                    if last:
                        t.then_inc(summed, 1)
                if not last:
                    t.then_inc(multiplied[s], 1)

            step(0, 0, True, False)
            step(1, 0, False, False)
            with pe.Fori(1, KF // 2 - 1) as it:
                step(0, it, False, False)
                step(1, it, False, False)
            step(0, KF // 2 - 1, False, False)
            step(1, KF // 2 - 1, False, True)

        @block.vector
        def _(dve):
            for its in sweep(dve, KF, [0, 0]):
                for k, s, u, it, other in its:
                    dve.wait_ge(multiplied[s], u)
                    dve.wait_ge(w_hi_ready[s], u + 1)
                    dve.tensor_tensor(w_lo[:, s, 512:D], w_raw[:, s, 512:D], w_hi[:, s, 512:D].bitcast(F32),
                                      ALU.subtract).then_inc(w2_lo_ready[s], 1)
                    dve.wait_ge(h_hi_ready[s], u + 1)
                    dve.tensor_tensor(h_lo[:, s, :], h_raw[:, s, :], h_hi[:, s, :].bitcast(F32),
                                      ALU.subtract).then_inc(h_lo_ready[s], 1)
            dve.wait_ge(x_in, 16)
            for m in range(KD):
                dve.wait_ge(summed, m + 1)
                gate = G.MOD[:, layer, 5 * KD + m:5 * KD + m + 1, v]
                dve.scalar_tensor_tensor(out=x[:, m, :], in0=acc[:, m, 0:T], scalar=gate, in1=x[:, m, :],
                                         op0=ALU.mult, op1=ALU.add).then_inc(added, 1)


class Tile:

    def __init__(self, q0, keys, kind=None):
        self.q0, self.kind = q0, kind
        self.pieces, self.kts, col = [], [], 0
        for a, n in keys:
            self.pieces.append((col, a, n))
            for o in range(0, n, P):
                self.kts.append((col + o, (a + o) // P, min(P, n - o)))
            col += n
        self.cols = col

    def score_parts(self, base):
        for col, tok, n in self.pieces:
            while n:
                m = min(n, 512 - (base + col) % 512)
                yield col, tok, m
                col, tok, n = col + m, tok + m, n - m


def attention(nc, G, name, mode, tiles, groups, q_src, k_src, v_src, q_toks, out, out_toks, IN=None):
    UNITS = 4
    mla, diff, swa, na = mode == "mla", mode == "diff", mode == "swa", mode == "na"
    rows = C_DQK if mla else P
    tq0, tq1 = q_toks
    TQ = tq1 - tq0
    nraw = 2 if mla else 1
    nw = 1 if diff else 2
    gs = max(len(g) for g in groups)
    kmax = max(len(t.kts) for t in tiles)
    smax = max(t.cols for t in tiles)
    NTL = len(tiles)
    N = UNITS * NTL
    group_of = {i: (g, p) for g, gr in enumerate(groups) for p, i in enumerate(gr)}
    with Stage(nc, name) as st:
        q_raw, k_raw, v_raw = st.sb("q_raw", [P, nraw, TQ]), st.sb("k_raw", [P, nraw, NT]), st.sb("v_raw", [P, NT])
        kpar = 1 if swa else 2
        if mla:
            QA, QB = st.sb("QH", [P, 2, 2, TQ], F32R), st.sb("QL", [P, 2, 2, TQ], F32R)
        else:
            QA = st.sb("QS", [P, 2, 2, TQ], F32R)
        KA, KB = st.sb("KA", [P, kpar, 2, NT], F32R), st.sb("KB", [P, kpar, 2, NT], F32R)
        V = st.sb("V", [P, kpar, NT // P, P])
        npr = 3
        PR = st.sb("PR", [P, npr, 2, smax])
        PT = st.sb("PT", [P, nw, kmax, 2 * gs * P])
        if nw == 2:
            diag = st.sb("diag", [P, 2, 2, P])
        opar = 2
        ob = st.sb("ob", [P, opar, NTL * P])
        stat = st.sb("stat", [P, 2, 8])
        if na:
            bias = st.sb("bias", [P, 2, 2, 5, CTX + NA_KEYS])
        if swa:
            mask = st.sb("mask", [P, 3, CTX + 3 * P])
        sw = 1536 if smax > 1024 else 1024
        NB = 8 - 2 * sw // 512
        sc = st.ps("sc", [P, 2, sw])
        tb = st.ps("tb", [P, NB, 512])
        q_in, k_in, v_in = st.sem("q_in"), st.sem("k_in"), st.sem("v_in")
        first_hi, first_lo, split = st.sem("first_hi"), st.sems("first_lo"), st.sem("split")
        mask_in, bias_in, bias_zero = st.sem("mask_in"), st.sems("bias_in"), st.sem("bias_zero")
        scored, maxed, exped, weighted = st.sems("scored"), st.sems("maxed"), st.sems("exped"), st.sems("weighted")
        t_ready, t_free = st.sems("t_ready", NB), st.sems("t_free", NB)
        chain, sink_exp, inverted = st.sem("chain"), st.sem("sink_exp"), st.sem("inverted")
        stored = st.sem("stored")
        block = st.block()

        def hi_parts(u, e):
            kp = 0 if swa else u % 2
            if mla:
                return [(QA[0:rows, u % 2, e, :], q_raw[0:rows, e, :]), (KA[0:rows, kp, e, :], k_raw[0:rows, e, :])]
            own, oth = slice(e * 64, e * 64 + 64), slice(64 - e * 64, P - e * 64)
            parts = [(QA[own, u % 2, e, :], q_raw[own, 0, :])]
            if not swa or u == 0:
                parts += [(KA[own, kp, e, :], k_raw[own, 0, :]), (KA[oth, kp, e, :], k_raw[own, 0, :])]
            return parts

        def lo_parts(u, e):
            kp = 0 if swa else u % 2
            if mla:
                return [(QB[0:rows, u % 2, e, :], q_raw[0:rows, e, :], QA[0:rows, u % 2, e, :]),
                        (KB[0:rows, kp, e, :], k_raw[0:rows, e, :], KA[0:rows, kp, e, :])]
            own, oth = slice(e * 64, e * 64 + 64), slice(64 - e * 64, P - e * 64)
            parts = [(QA[oth, u % 2, e, :], q_raw[own, 0, :], QA[own, u % 2, e, :])]
            if not swa or u == 0:
                parts += [(KB[x, kp, e, :], k_raw[own, 0, :], KA[own, kp, e, :]) for x in (own, oth)]
            return parts

        n_first = len(hi_parts(0, 0))
        n_unit = 4 * len(hi_parts(1, 0))

        def wait_split(eng, u, e):
            if u == 0:
                eng.wait_ge(first_hi, n_first * (e + 1))
                eng.wait_ge(first_lo[e], n_first)
            else:
                eng.wait_ge(split, n_unit * (u - 1) + n_unit // 2 * (e + 1))

        def bank_jobs(n):
            before, after = [], []
            if 2 <= n < N + 2:
                kts = tiles[(n - 2) % NTL].kts
                for e in range(nw):
                    full = [k for k in range(len(kts)) if kts[k][2] == P]
                    jobs = [("p", n - 2, e, full[c:c + 4]) for c in range(0, len(full), 4)]
                    jobs += [("p", n - 2, e, [k]) for k in range(len(kts)) if kts[k][2] < P]
                    if e == 0:
                        before, after = (jobs[:2], jobs[2:]) if diff else (jobs, [])
                    else:
                        after = after + jobs
            if n >= 3 and group_of[(n - 3) % NTL][1] == len(groups[group_of[(n - 3) % NTL][0]]) - 1:
                after.insert(0, ("o", group_no(n - 3), 0, 0))
            if n == 0:
                after += [("v", 0, 0, c) for c in range(3)]
            elif not swa and n % NTL == 5 and n // NTL + 1 < UNITS:
                after += [("v", n // NTL + 1, 0, c) for c in range(3)]
            return before, after

        def group_no(m):
            u, i = divmod(m, NTL)
            return u * len(groups) + group_of[i][0]

        number, uses = {}, 0
        for n in range(N + 3):
            for kind, a, e, c in bank_jobs(n)[0] + bank_jobs(n)[1]:
                number[kind, a, e] = uses
                uses += 1

        def wait_ready(eng, kind, a, e=0):
            eng.wait_ge(t_ready[number[kind, a, e] % NB], number[kind, a, e] // NB + 1)

        def wait_freed(eng, kind, a, e=0):
            eng.wait_ge(t_free[number[kind, a, e] % NB], number[kind, a, e] // NB + 1)

        def pt_cols(m):
            u, i = divmod(m, NTL)
            p = group_no(m) % 2 * gs + group_of[i][1]
            return p * P, (p + 1) * P

        @block.sync
        def _(sp):
            if swa:
                sp.dma_start(mask[:, :, :], IN["k_swa_mask"]).then_inc(mask_in, 16)

            def store(u):
                for g in range(len(groups)):
                    wait_freed(sp, "o", u * len(groups) + g)
                sp.dma_start(out[u * P:(u + 1) * P, out_toks[0]:out_toks[1]], ob[:, u % opar, :]).then_inc(stored, 16)

            for u in range(UNITS):
                if u >= 1:
                    for e in range(2):
                        wait_split(sp, u - 1, e)
                for r in range(nraw):
                    sp.dma_start(q_raw[0:rows, r, :], q_src(u, r)[:, tq0:tq1]).then_inc(q_in, 16)
                    if not swa or u == 0:
                        sp.dma_start(k_raw[0:rows, r, :], k_src(u, r)).then_inc(k_in, 16)
                if not swa or u == 0:
                    if u >= 1:
                        wait_ready(sp, "v", u - 1, 0)
                    sp.dma_start(v_raw[:, :], v_src(u)).then_inc(v_in, 16)
                if na:
                    if u >= 2:
                        sp.wait_ge(maxed[0], NTL * (u - 1))
                        sp.wait_ge(maxed[1], NTL * (u - 1))
                    for e in range(2):
                        for kind in range(5):
                            for rr in range(2):
                                skip = rr if NA_ROWS[kind] == 9 else 0
                                d0 = NA_D0[kind] - rr + skip
                                src = G.RPB[2 * u + e, d0:d0 + NA_H, :, :].rearrange("d c k -> c d k")
                                c0 = CTX + skip * GRID_W
                                dst = bias[rr * 64:rr * 64 + 64, u % 2, e, kind, c0:c0 + NA_H * GRID_W]
                                sp.dma_start(dst.rearrange("p (d k) -> p d k", k=64), src).then_inc(bias_in[u % 2], 16)
                if u >= 1:
                    store(u - 1)
            store(UNITS - 1)
            sp.wait_ge(stored, 16 * UNITS)

        @block.gpsimd
        def _(pool):
            if na:
                pool.memset(bias[:, :, :, :, 0:CTX], 0.0).then_inc(bias_zero, 1)
                for rr in range(2):
                    c0 = CTX + (0 if rr else NA_H * GRID_W)
                    pool.wait_ge(bias_zero, rr + 1)
                    pool.memset(bias[rr * 64:rr * 64 + 64, :, :, 2, c0:c0 + GRID_W], NEG).then_inc(bias_zero, 1)
            pool.wait_ge(first_hi, 2 * n_first)
            for dst, raw, high in lo_parts(0, 1):
                pool.tensor_tensor(dst, raw, high.bitcast(F32), ALU.subtract).then_inc(first_lo[1], 1)
            for u in range(1, UNITS):
                pool.wait_ge(q_in, 16 * nraw * (u + 1))
                if not swa:
                    pool.wait_ge(k_in, 16 * nraw * (u + 1))
                if u >= 2:
                    for e in range(2):
                        pool.wait_ge(scored[e], NTL * (u - 1))
                for e in range(2):
                    for dst, raw in hi_parts(u, e):
                        pool.tensor_copy(dst, raw).then_inc(split, 1)
                    pool.wait_ge(split, n_unit * (u - 1) + n_unit // 4 * (2 * e + 1))
                    for dst, raw, high in lo_parts(u, e):
                        pool.tensor_tensor(dst, raw, high.bitcast(F32), ALU.subtract).then_inc(split, 1)

        @block.tensor
        def _(pe):
            job = [0]

            def scores(n, e):
                u, i = divmod(n, NTL)
                t = tiles[i]
                ku, ke = (0, u // 2) if swa else (u % 2, e)
                wait_split(pe, u, e)
                if swa:
                    wait_split(pe, 0, ke)
                if n:
                    pe.wait_ge(maxed[e] if tiles[(n - 1) % NTL].kind is not None else exped[e], n)
                q = slice(t.q0 - tq0, t.q0 - tq0 + P)
                for col, tok, m in t.score_parts(0):
                    o = sc[:, e, col:col + m]
                    if mla:
                        work = [(QA, KA), (QA, KB), (QB, KA)]
                    else:
                        work = [(QA, KA), (QA, KB)]
                    for j, (a, b) in enumerate(work):
                        last = pe.matmul(o, a[0:rows, u % 2, e, q], b[0:rows, ku, ke, tok:tok + m], start=j == 0,
                                         stop=j == len(work) - 1)
                last.then_inc(scored[e], 1)

            def turn(jobs):
                for kind, a, e, c in jobs:
                    bank, use = job[0] % NB, job[0] // NB
                    pe.wait_ge(t_free[bank], use)
                    if kind == "o":
                        values(a, bank)
                    elif kind == "v":
                        pe.wait_ge(v_in, 16 * (a + 1))
                        for k in range(4 * c, min(4 * c + 4, NT // P)):
                            last = pe.transpose(tb[:, bank, (k % 4) * P:(k % 4 + 1) * P], v_raw[:, k * P:(k + 1) * P],
                                                G.IDENT[:, :])
                        last.then_inc(t_ready[bank], 1)
                    else:
                        pe.wait_ge(weighted[e], a + 1)
                        t = tiles[a % NTL]
                        for x, k in enumerate(c):
                            col, _, ln = t.kts[k]
                            w = PR[:, a % npr, e, col:col + ln]
                            o = tb[0:ln, bank, x * P:(x + 1) * P]
                            if diff:
                                last = pe.transpose(o, w, G.IDENT[:, :])
                            else:
                                last = pe.matmul(o, w, diag[:, a % 2, e, :], start=True, stop=True)
                        last.then_inc(t_ready[bank], 1)
                    job[0] += 1

            def values(gn, bank):
                u, g = divmod(gn, len(groups))
                members = groups[g]
                m = u * NTL + members[-1]
                for x in range(u * NTL + members[0], m + 1):
                    for e in range(nw):
                        for bk in range(NB):
                            done = max([0] + [k // NB + 1 for k in tile_uses[x] if k % NB == bk])
                            if done:
                                pe.wait_ge(t_free[bk], done)
                c0 = pt_cols(u * NTL + members[0])[0]
                c1 = c0 + len(members) * P
                t = tiles[members[0]]
                for e in range(nw):
                    h = slice(0, P) if diff else slice(e * 64, e * 64 + 64)
                    vc = slice(u // 2 * 64, u // 2 * 64 + 64) if swa else h
                    for k, (_, vt, ln) in enumerate(t.kts):
                        last = pe.matmul(tb[h, bank, 0:c1 - c0], V[0:ln, 0 if swa else u % 2, vt, vc], PT[0:ln, e, k, c0:c1],
                                         start=k == 0, stop=k == len(t.kts) - 1)
                last.then_inc(t_ready[bank], 1)

            tile_uses, number_ = {}, 0
            for n in range(N + 3):
                for kind, a, e, c in bank_jobs(n)[0] + bank_jobs(n)[1]:
                    if kind == "p":
                        tile_uses.setdefault(a, []).append(number_)
                    number_ += 1
            for n in range(N + 3):
                for half in range(2):
                    if n < N:
                        scores(n, half)
                    turn(bank_jobs(n)[half])

        def evacuate(eng, copy, jobs, job):
            for what, a, e, c in jobs:
                bank, use = job[0] % NB, job[0] // NB
                job[0] += 1
                if bank % 2 != (0 if copy == "act" else 1):
                    continue
                eng.wait_ge(t_ready[bank], use + 1)
                if what == "v":
                    ks = range(4 * c, min(4 * c + 4, NT // P))
                    if a >= 2:
                        wait_ready(eng, "o", len(groups) * (a - 1) - 1)
                    dst = V[:, 0 if swa else a % 2, ks[0]:ks[-1] + 1, :]
                    src = tb[:, bank, 0:len(ks) * P].rearrange("p (k c) -> p k c", c=P)
                elif what == "o":
                    u, g = divmod(a, len(groups))
                    if u >= opar:
                        eng.wait_ge(stored, 16 * (u - opar + 1))
                    dst = ob[:, u % opar, groups[g][0] * P:(groups[g][-1] + 1) * P]
                    src = tb[:, bank, 0:len(groups[g]) * P]
                else:
                    ln = tiles[a % NTL].kts[c[0]][2]
                    before = group_no(a) - 2
                    if before >= 0:
                        wait_ready(eng, "o", before)
                    c0, c1 = pt_cols(a)
                    dst = PT[0:ln, e, c[0]:c[-1] + 1, c0:c1]
                    src = tb[0:ln, bank, 0:len(c) * P].rearrange("p (k c) -> p k c", c=P)
                if copy == "act":
                    eng.activation(dst, src, ACT.Copy).then_inc(t_free[bank], 1)
                else:
                    eng.tensor_copy(dst, src).then_inc(t_free[bank], 1)

        @block.scalar
        def _(act):
            job = [0]

            act.wait_ge(q_in, 16 * nraw)
            act.wait_ge(k_in, 16 * nraw)
            for e in range(2):
                for dst, raw in hi_parts(0, e):
                    act.activation(dst, raw, ACT.Copy).then_inc(first_hi, 1)
            for n in range(N + 3):
                if diff and 1 <= n <= N:
                    m = n - 1
                    w = PR[:, m % npr, 1, 0:tiles[m % NTL].cols]
                    act.wait_ge(inverted, m + 1)
                    act.activation(w, w, ACT.Copy, scale=stat[:, m % 2, 3:4]).then_inc(weighted[1], 1)
                for e in range(2):
                    if n < N:
                        t = tiles[n % NTL]
                        act.wait_ge(maxed[e], n + 1)
                        if n >= npr and nw > e:
                            wait_ready(act, "p", n - npr, e)
                        elif n >= npr:
                            act.wait_ge(weighted[0], n - npr + 1)
                        src = PR[:, n % npr, e, 0:t.cols] if t.kind is not None else sc[:, e, 0:t.cols]
                        act.activation(PR[:, n % npr, e, 0:t.cols], src, ACT.Exp, bias=stat[:, n % 2, e:e + 1],
                                       accum_out=stat[:, n % 2, 2 + e:3 + e]).then_inc(exped[e], 1)
                    if swa and e == 1 and n < N:
                        act.activation(stat[:, n % 2, 6:8], stat[:, n % 2, 4:6], ACT.Exp).then_inc(sink_exp, 1)
                    evacuate(act, "act", bank_jobs(n)[e], job)

        @block.vector
        def _(dve):
            job = [0]
            links = [0]

            def link(ins):
                links[0] += 1
                ins.then_inc(chain, 1)
                dve.wait_ge(chain, links[0])

            def invert(m):
                p = m % 2
                for e in range(2):
                    dve.wait_ge(exped[e], m + 1)
                s = stat[:, p, 2:4]
                if swa:
                    dve.wait_ge(sink_exp, m + 1)
                    link(dve.tensor_tensor(s, s, stat[:, p, 6:8], ALU.add))
                link(dve.reciprocal(s, s))
                if not diff:
                    for e in range(2):
                        if m >= 2:
                            wait_ready(dve, "p", m - 2, e)
                        dve.tensor_scalar(diag[:, p, e, :], G.IDENT[:, :], stat[:, p, 2 + e:3 + e], None, ALU.mult)\
                            .then_inc(weighted[e], 1)
                    return
                link(dve.tensor_scalar(stat[:, p, 2:3], stat[:, p, 2:3], G.LINV[:, 0:1], None, ALU.mult))
                dve.tensor_scalar(stat[:, p, 3:4], stat[:, p, 3:4], G.NLAM[:, 0:1], None, ALU.mult).then_inc(inverted, 1)

            def weigh(m):
                p, pr, cols = m % 2, m % npr, tiles[m % NTL].cols
                dve.wait_ge(weighted[1], m + 1)
                w = PR[:, pr, 0, 0:cols]
                dve.scalar_tensor_tensor(out=w, in0=w, scalar=stat[:, p, 2:3], in1=PR[:, pr, 1, 0:cols],
                                         op0=ALU.mult, op1=ALU.add).then_inc(weighted[0], 1)

            def biased_max(n, e):
                u, i = divmod(n, NTL)
                t = tiles[i]
                if na:
                    dve.wait_ge(bias_in[u % 2], 20 * 16 * (u // 2 + 1))
                dve.wait_ge(scored[e], n + 1)
                if n >= 2:
                    dve.wait_ge(exped[e], n - 1)
                s = sc[:, e, 0:t.cols]
                mx = stat[:, n % 2, e:e + 1]
                if t.kind is None:
                    dve.tensor_reduce(mx, s, AX, ALU.max, negate=True).then_inc(maxed[e], 1)
                    return
                if n >= npr:
                    wait_ready(dve, "p", n - npr, e)
                tab = bias[:, u % 2, e, t.kind, 0:t.cols] if na else mask[:, t.kind, 0:t.cols]
                link(dve.tensor_tensor_reduce(PR[:, n % npr, e, 0:t.cols], s, tab, 1.0, -3e38, ALU.add, ALU.max, mx))
                if swa:
                    sink = G.SINK[:, 2 * u + e:2 * u + e + 1]
                    link(dve.tensor_tensor(mx, mx, sink, ALU.max))
                    if n >= 2:
                        dve.wait_ge(sink_exp, n - 1)
                    link(dve.tensor_tensor(stat[:, n % 2, 4 + e:5 + e], sink, mx, ALU.subtract))
                dve.tensor_scalar(mx, mx, -1.0, None, ALU.mult).then_inc(maxed[e], 1)

            dve.wait_ge(first_hi, n_first)
            for dst, raw, high in lo_parts(0, 0):
                dve.tensor_tensor(dst, raw, high.bitcast(F32), ALU.subtract).then_inc(first_lo[0], 1)
            if swa:
                dve.wait_ge(mask_in, 16)
            if na:
                dve.wait_ge(bias_zero, 3)
            for n in range(N + 3):
                if 1 <= n <= N:
                    invert(n - 1)
                for e in range(2):
                    if n < N:
                        biased_max(n, e)
                    if diff and e == 1 and 1 <= n <= N:
                        weigh(n - 1)
                    evacuate(dve, "dve", bank_jobs(n)[e], job)


def transpose_out(nc, G, out):
    with Stage(nc, "xout") as st:
        xt = st.sb("xt", [P, 2, KD, P])
        tok = st.sb("tok", [P, 2, D])
        tps = st.ps("tps", [P, 2, KD, P])
        load, turn, copy_a, copy_v, store = (st.sems(n) for n in ("load", "turn", "copy_a", "copy_v", "store"))
        block = st.block()
        O = out.rearrange("a (t p) d -> (a t) p d", p=P)
        XT = G.X.rearrange("(k p) t -> p k t", p=P)
        n = LAT // P

        @block.sync
        def _(sp):
            for its in sweep(sp, n, [0, 0]):
                for m, s, u, it, other in its:
                    sp.wait_ge(turn[s], u)
                    sp.dma_start(xt[:, s, :, :], XT[:, :, bass.ds(CTX + m * P, P)]).then_inc(load[s], 16)

        @block.tensor
        def _(pe):
            for its in sweep(pe, n, [0, 0]):
                for m, s, u, it, other in its:
                    pe.wait_ge(load[s], 16 * u + 16)
                    pe.wait_ge(copy_a[s], u)
                    pe.wait_ge(copy_v[s], u)
                    for k in range(KD):
                        t = pe.transpose(tps[:, s, k, :], xt[:, s, k, :], G.IDENT[:, :])
                    t.then_inc(turn[s], 1)

        @block.scalar
        def _(act):
            used = [0, 0]
            for its in sweep(act, n, used):
                for m, s, u, it, other in its:
                    act.wait_ge(turn[s], u + 1)
                    act.wait_ge(store[s], 16 * u)
                    act.activation(tok[:, s, 0:512], tps[:, s, 0:4, :].rearrange("p a b -> p (a b)"), ACT.Copy).then_inc(copy_a[s], 1)
                    act.wait_ge(copy_a[s], u + 1)
                    act.wait_ge(copy_v[s], u + 1)
                    act.dma_start(O[bass.ds(m, 1)].rearrange("a p d -> (a p) d"), tok[:, s, :]).then_inc(store[s], 16)
            for s in range(2):
                act.wait_ge(store[s], 16 * used[s])

        @block.vector
        def _(dve):
            for its in sweep(dve, n, [0, 0]):
                for m, s, u, it, other in its:
                    dve.wait_ge(turn[s], u + 1)
                    dve.wait_ge(store[s], 16 * u)
                    dve.tensor_copy(tok[:, s, 512:1024], tps[:, s, 4:8, :].rearrange("p a b -> p (a b)")).then_inc(copy_v[s], 1)


class Globals:
    pass


def trunk(nc, IN, out, stop=99):
    G = Globals()
    Stage.cleared = []
    ctx = ExitStack()
    with ctx:
        def sb(name, shape, dt=F32):
            return ctx.enter_context(nc.sbuf_tensor(name, shape, dt))

        def dram(name, shape):
            return nc.dram_tensor(name, shape, F32, kind="Internal").ap()

        G.IDENT, G.BLK64, G.ONES = sb("IDENT", [P, P]), sb("BLK64", [P, P]), sb("ONES", [P, P])
        G.ROT, G.ROT96, G.ROTG = sb("ROT", [P, P]), sb("ROT96", [C_DQK, C_DQK]), sb("ROTG", [P, 6, P])
        G.LINV, G.EPSL = sb("LINV", [P, 1]), sb("EPSL", [P, 1])
        G.EPSC, G.NLAM, G.SINK, G.CVEC = sb("EPSC", [P, 1]), sb("NLAM", [P, 1]), sb("SINK", [P, 8]), sb("CVEC", [P, 16])
        G.GV, G.PRM = sb("GV", [P, GV_N]), sb("PRM", [P, PRM_N])
        G.MOD, G.GS = sb("MOD", [P, DEPTH, 6 * KD, 2]), sb("GS", [P, DEPTH, 2, KD, 2])
        G.X, G.Y, G.Z, G.H = dram("X", [D, NT]), dram("Y", [3072, NT]), dram("Z", [D, NT]), dram("H", [FFN, NT])
        G.RPB = dram("RPB", [8, HALF_ROWS, GRID_W, GRID_W])
        G.Q, G.K, G.VM = dram("Q", [C_HEADS * C_DQK, NT]), dram("K", [C_HEADS * C_DQK, NT]), dram("VM", [512, NT])
        G.Y1 = dram("Y1", [1440, NT])

        load_parameters(nc, G, IN)
        for layer in range(DEPTH):
            modulation(nc, G, IN, layer)
        transpose_in(nc, G, IN)
        if stop <= 1:
            return

        def modulated(layer, which, t0):
            rs = [(v, max(a, t0), b) for v, a, b in ((1, 0, CTX), (0, CTX, NT)) if b > t0]
            scale = lambda k: [(G.GS[:, layer, which, k, v:v + 1], a, b) for v, a, b in rs]
            shift = lambda k: [(G.MOD[:, layer, 3 * which * KD + k, v:v + 1], a, b) for v, a, b in rs]
            return dict(scale=scale, shift=shift)

        def gain(col, t0, limit=99):
            return lambda k: [(G.GV[:, col + (k if limit == 99 else 0):col + (k if limit == 99 else 0) + 1], t0, NT)] if k < limit else []

        def ffn(layer, t0):
            with Stage(nc, f"fa{layer}") as st:
                act_h, act_l = st.sb("act_h", [P, KD, NT - t0], F32R), st.sb("act_l", [P, KD, NT - t0], F32R)
                operand(nc, G, f"f{layer}", G.X, KD, t0, NT, act_h, act_l, **modulated(layer, 1, t0))
                ffn_up(nc, G, f"up{layer}", IN["ffn_up"][layer], act_h, act_l, t0, layer, (t0, NT), G.H)
            for i, (a, b) in enumerate(([(0, CTX)] if t0 == 0 else []) + chunks(CTX, NT)):
                ffn_down(nc, G, f"dn{layer}{i}", IN["ffn_down"][layer], G.H, layer, (a, b))

        with Stage(nc, "a0") as st:
            act_h, act_l = st.sb("act_h", [P, KD, NT], F32R), st.sb("act_l", [P, KD, NT], F32R)
            operand(nc, G, "m0", G.X, KD, 0, NT, act_h, act_l, **modulated(0, 0, 0))
            both = (0, NT)
            heads = dict(mw=P, toks=both, rows=P, own=P, ones=G.BLK64, width=64)
            at = lambda c0: (lambda m, s, it: c0 + m * P)
            segs = [dict(heads, tiles=4, col=at(0), row=0, rope=G.ROTG[:, 0, :], gain=GV_AQ),
                    dict(heads, tiles=4, col=at(512), row=512, rope=G.ROTG[:, 1, :], gain=GV_AK),
                    dict(heads, tiles=4, col=at(1536), row=1536, rope=None, gain=GV_BQ),
                    dict(heads, tiles=4, col=at(2048), row=2048, rope=None, gain=GV_BK)]
            project_heads(nc, G, "qk0", IN["ev_w_in"][0], KD, act_h, act_l, 0, segs, G.Y, (IN["k_cos"], IN["k_sin"]))
            vsegs = [dict(mw=P, toks=both, tiles=4, col=at(1024), row=1024),
                     dict(mw=P, toks=both, tiles=4, col=at(2560), row=2560)]
            project_store(nc, G, "v0", IN["ev_w_in"][0], KD, act_h, act_l, 0, vsegs, G.Y)
        if stop <= 2:
            return
        whole = [(0, NT)]
        ctx_tiles = [Tile(q, [(0, CTX)]) for q in range(0, CTX, P)]
        lat_tiles = [Tile(q, whole) for q in range(CTX, NT, P)]
        nlat = LAT // P
        row = lambda src, r0: (lambda u, r=0: src[r0 + u * P:r0 + u * P + P])
        attention(nc, G, "da", "diff", ctx_tiles + lat_tiles, [[i, i + 1] for i in range(0, 2 + nlat, 2)],
                  row(G.Y, 0), row(G.Y, 512), row(G.Y, 1024), (0, NT), G.Z[0:512], (0, NT))
        if stop <= 3:
            return
        na_tiles = []
        for i in range(nlat):
            kind = NA_KIND[i]
            r0 = NA_D0[kind] + 2 * i - 7
            na_tiles.append(Tile(CTX + i * P, [(0, CTX), (CTX + r0 * GRID_W, NA_ROWS[kind] * GRID_W)], kind))
        attention(nc, G, "na", "na", ctx_tiles + na_tiles, [[i] for i in range(2 + nlat)],
                  row(G.Y, 1536), row(G.Y, 2048), row(G.Y, 2560), (0, NT), G.Z[512:1024], (0, NT), IN)
        if stop <= 4:
            return
        with Stage(nc, "o0") as st:
            act_h, act_l = st.sb("act_h", [P, KD, NT], F32R), st.sb("act_l", [P, KD, NT], F32R)
            operand(nc, G, "z0", G.Z, KD, 0, NT, act_h, act_l, norm=False, sub_tiles=4, mean_over=P,
                    scale=gain(GV_SUB, 0, 4))
            project_residual(nc, G, "out0", IN["ev_w_out"][0], KD, act_h, act_l, 0, 0, (0, NT), 2)
        if stop <= 5:
            return
        ffn(0, 0)
        if stop <= 6:
            return

        with Stage(nc, "a1") as st:
            act_h, act_l = st.sb("act_h", [P, KD, NT], F32R), st.sb("act_l", [P, KD, NT], F32R)
            operand(nc, G, "m1", G.X, KD, 0, NT, act_h, act_l, **modulated(1, 0, 0))
            lat = (CTX, NT)
            heads = dict(mw=P, rows=P, own=P, ones=G.BLK64, width=64)
            segs = [dict(heads, toks=lat, tiles=4, col=at(ODD_DQ), row=ODD_DQ, rope=G.ROTG[:, 2, :], gain=GV_DQ),
                    dict(heads, toks=both, tiles=1, col=at(ODD_DK), row=ODD_DK, rope=G.ROTG[:, 3, :], gain=GV_DK)]
            project_heads(nc, G, "qk1", IN["od_w_in"][0], KD, act_h, act_l, 0, segs, G.Y1, (IN["k_cos"], IN["k_sin"]))
            ssegs = [dict(mw=P, toks=lat, tiles=3, col=at(ODD_CQ), row=ODD_CQ),
                     dict(mw=P, toks=both, tiles=2, col=at(ODD_CKV), row=ODD_CKV),
                     dict(mw=P, toks=both, tiles=1, col=at(ODD_DV), row=ODD_DV),
                     dict(mw=C_ROPE, toks=both, tiles=1, col=at(ODD_CKR), row=ODD_CKR)]
            project_store(nc, G, "s1", IN["od_w_in"][0], KD, act_h, act_l, 0, ssegs, G.Y1)
        if stop <= 7:
            return
        t96 = (IN["k_cos96"], IN["k_sin96"])
        with Stage(nc, "a2") as st:
            act_h, act_l = st.sb("act_h", [P, 3, LAT], F32R), st.sb("act_l", [P, 3, LAT], F32R)
            operand(nc, G, "cq", G.Y1[0:Q_LORA], 3, CTX, NT, act_h, act_l, mean_over=Q_LORA, scale=gain(GV_CQA, CTX))
            segs = [dict(mw=C_DQK, toks=lat, tiles=8, col=lambda m, s, it: m * C_DQK, row=0, rows=C_DQK, own=C_DQK,
                         ones=G.ONES, width=C_DQK, rope=G.ROTG[0:C_DQK, 4, :], gain=GV_CQ)]
            project_heads(nc, G, "mq", IN["c_w_qb"][0], 3, act_h, act_l, CTX, segs, G.Q, t96)
        with Stage(nc, "a3") as st:
            act_h, act_l = st.sb("act_h", [P, 2, NT], F32R), st.sb("act_l", [P, 2, NT], F32R)
            operand(nc, G, "ck", G.Y1[ODD_CKV:ODD_CKR], 2, 0, NT, act_h, act_l, mean_over=KV_LORA, scale=gain(GV_CKVA, 0))
            segs = [dict(mw=P, toks=both, tiles=8, col=at(0), row=0, rows=C_DQK, own=64,
                         ones=G.ONES, width=C_DQK, rope=G.ROTG[0:C_DQK, 5, :], gain=GV_CK)]
            project_heads(nc, G, "mk", IN["c_w_kvb"][0], 2, act_h, act_l, 0, segs, G.K, t96,
                          kr=G.Y1[ODD_CKR:ODD_DQ], v_out=G.VM)
        if stop <= 8:
            return
        head = lambda src: (lambda u, r: src[(2 * u + r) * C_DQK:(2 * u + r + 1) * C_DQK])
        attention(nc, G, "ma", "mla", lat_tiles, [[i, i + 1] for i in range(0, nlat, 2)], head(G.Q), head(G.K), row(G.VM, 0),
                  lat, G.Z[0:512], lat)
        if stop <= 9:
            return
        swa_tiles = []
        for i in range(nlat):
            a, b = max(0, (i - 1) * P), min(LAT, (i + 2) * P)
            swa_tiles.append(Tile(CTX + i * P, [(0, CTX), (CTX + a, b - a)], 0 if i == 0 else 2 if i == nlat - 1 else 1))
        one = lambda r0: (lambda u, r=0: G.Y1[r0:r0 + P])
        attention(nc, G, "sw", "swa", swa_tiles, [[i] for i in range(nlat)], row(G.Y1, ODD_DQ), one(ODD_DK), one(ODD_DV),
                  lat, G.Z[512:1024], lat, IN)
        if stop <= 10:
            return
        with Stage(nc, "o1") as st:
            act_h, act_l = st.sb("act_h", [P, KD, LAT], F32R), st.sb("act_l", [P, KD, LAT], F32R)
            operand(nc, G, "z1", G.Z, KD, CTX, NT, act_h, act_l, norm=False)
            project_residual(nc, G, "out1", IN["od_w_out"][0], KD, act_h, act_l, CTX, 1, lat, 2)
        ffn(1, CTX)
        transpose_out(nc, G, out)


def shape_constants():
    f = np.float32
    k = {"k_ident": np.eye(P, dtype=f)}
    blk = np.zeros((P, P), f)
    rot = np.zeros((P, P), f)
    for h in (0, 64):
        blk[h:h + 64, h:h + 64] = 1
        for i in range(32):
            rot[h + 32 + i, h + i] = -1
            rot[h + i, h + 32 + i] = 1
    rot96 = np.zeros((C_DQK, C_DQK), f)
    for i in range(C_ROPE // 2):
        rot96[80 + i, 64 + i] = -1
        rot96[64 + i, 80 + i] = 1
    k["k_blk64"], k["k_rot"], k["k_rot96"] = blk, rot, rot96

    def angles(dim):
        t = np.arange(LAT)
        quarter = dim // 4
        inv = (f(10000.0) ** (-np.arange(quarter, dtype=f) / f(quarter))).astype(f)
        ang = np.concatenate([(t // GRID_W).astype(f)[:, None] * inv, (t % GRID_W).astype(f)[:, None] * inv], -1)
        return np.cos(ang).T.astype(f), np.sin(ang).T.astype(f)

    c, s = angles(64)
    cos, sin = np.ones((P, NT), f), np.zeros((P, NT), f)
    for r in range(0, P, 32):
        cos[r:r + 32, CTX:], sin[r:r + 32, CTX:] = c, s
    c, s = angles(C_ROPE)
    cos96, sin96 = np.ones((C_DQK, NT), f), np.zeros((C_DQK, NT), f)
    for r in (64, 80):
        cos96[r:r + 16, CTX:], sin96[r:r + 16, CTX:] = c, s
    k["k_cos"], k["k_sin"], k["k_cos96"], k["k_sin96"] = cos, sin, cos96, sin96

    q, j = np.arange(P)[:, None], np.arange(3 * P)[None, :]
    band = np.where(np.abs(j - P - q) <= P, f(0), f(NEG))
    swa = np.zeros((P, 3, CTX + 3 * P), f)
    swa[:, 0, CTX:CTX + 2 * P] = band[:, P:]
    swa[:, 1, CTX:] = band
    swa[:, 2, CTX:CTX + 2 * P] = band[:, :2 * P]
    k["k_swa_mask"] = swa
    return k


INPUTS = ["x", "c", "ctx", "c_ctx", "ada_w", "ada_b", "norm_mix", "norm_ffn", "ffn_up", "ffn_conv_w", "ffn_conv_b",
          "ffn_down", "ev_w_in", "ev_w_out", "a_q_norm", "a_k_norm", "a_lam_q1", "a_lam_k1", "a_lam_q2", "a_lam_k2",
          "a_subln", "b_q_norm", "b_k_norm", "b_rpb", "od_w_in", "od_w_out", "c_q_a_norm", "c_w_qb", "c_kv_a_norm",
          "c_w_kvb", "c_q_norm", "c_k_norm", "d_q_norm", "d_k_norm", "d_sink"]


def kernel(**inputs):
    import concourse.bacc as bacc
    from concourse.bass_utils import run_bass_kernel_spmd

    nc = bacc.Bacc("TRN2", target_bir_lowering=False, num_devices=1)
    arrays, args = {}, {}
    for name, a in [(n, inputs[n]) for n in INPUTS] + list(shape_constants().items()):
        a = np.ascontiguousarray(a)
        arrays[f"in_{name}"] = a
        args[name] = nc.dram_tensor(f"in_{name}", a.shape, mybir.dt.from_np(a.dtype), kind="ExternalInput").ap()
    out = nc.dram_tensor("out", (1, LAT, D), F32, kind="ExternalOutput").ap()
    trunk(nc, args, out)
    r = run_bass_kernel_spmd(nc, [arrays], core_ids=[0])
    return r.results[0]["out"]
```

```python
import math
from contextlib import ExitStack

import concourse.bass as bass
import numpy as np
from concourse import mybir

F32 = mybir.dt.float32
F32R = mybir.dt.float32r
ACT = mybir.ActivationFunctionType
ALU = mybir.AluOpType
AX = mybir.AxisListType.X

P = 128
D = 1024
KD = D // P
DEPTH = 2
LAT = 1024
CTX = 256
NT = CTX + LAT
GRID_W = 64
EPS = 1e-6
NEG = -1e30
FFN = 2816
KF = FFN // P
NA_H, NA_W = 8, 16
HALF_ROWS = 2 * NA_H - 1
HALF_COLS = 2 * NA_W - 1
LAM_INIT = (0.8 - 0.6 * math.exp(0.0))
C_HEADS, C_DQK = 8, 96
Q_LORA, KV_LORA, C_ROPE = 384, 256, 32
ODD_CQ, ODD_CKV, ODD_CKR = 0, Q_LORA, Q_LORA + KV_LORA
ODD_DQ = ODD_CKR + C_ROPE
ODD_DK = ODD_DQ + 512
ODD_DV = ODD_DK + P
PRM_NORM_MIX, PRM_NORM_FFN, PRM_ADA_B = 0, DEPTH * KD, 2 * DEPTH * KD
PRM_CONV_W = PRM_ADA_B + DEPTH * 6 * KD
PRM_CONV_B = PRM_CONV_W + DEPTH * 3 * 2 * KF
PRM_N = PRM_CONV_B + DEPTH * 2 * KF
GV_AQ, GV_AK, GV_BQ, GV_BK, GV_DQ, GV_DK, GV_CQ, GV_CK, GV_SUB, GV_CQA, GV_CKVA = 0, 1, 2, 3, 4, 5, 6, 7, 8, 9, 12
GV_N = 14
NA_KIND = [0, 1, 2, 2, 2, 2, 3, 4]
NA_D0 = [7, 5, 3, 3, 1]
NA_ROWS = [8, 8, 9, 8, 8]
NA_KEYS = 9 * GRID_W


def chunks(t0, t1, step=512):
    return [(a, min(a + step, t1)) for a in range(t0, t1, step)]


def sweep(eng, tiles, used, lag=False):
    pairs = tiles // 2

    def one(it):
        return [(2 * it, 0, it + used[0], it, it + used[1]), (2 * it + 1, 1, it + used[1], it, it + used[0] + 1)]

    first = min(pairs, (1 if used[0] == 0 else 0) + (1 if lag else 0))
    for it in range(first):
        yield one(it)
    if pairs - first == 1:
        yield one(first)
    elif pairs - first > 1:
        with eng.Fori(first, pairs) as it:
            yield one(it)
    used[0] += pairs
    used[1] += pairs
    if tiles % 2:
        yield [(tiles - 1, 0, used[0], pairs, used[1])]
        used[0] += 1


class Stage:
    cleared = []

    def __init__(self, nc, name):
        self.nc, self.name, self.ctx, self.own = nc, name, ExitStack(), []

    def __enter__(self):
        return self

    def __exit__(self, *a):
        self.ctx.__exit__(*a)
        if self.own:
            for h in Stage.cleared:
                self.nc.release_semaphore(h)
            for h in self.own:
                self.nc.gpsimd.sem_clear(h)
            Stage.cleared = self.own

    def sb(self, name, shape, dt=F32):
        return self.ctx.enter_context(self.nc.sbuf_tensor(f"{self.name}_{name}", shape, dt))

    def ps(self, name, shape, dt=F32):
        return self.ctx.enter_context(self.nc.psum_tensor(f"{self.name}_{name}", shape, dt))

    def sem(self, name):
        self.own.append(self.nc.alloc_semaphore(f"{self.name}_{name}"))
        return self.own[-1]

    def sems(self, name, n=2):
        return [self.sem(f"{name}{i}") for i in range(n)]

    def block(self):
        return self.ctx.enter_context(self.nc.Block())


def load_parameters(nc, G, IN):
    with Stage(nc, "par") as st:
        rows = st.sb("rows", [P, 5, P])
        vec = st.sb("vec", [16, P])
        svec = st.sb("svec", [16, P])
        lamv = st.sb("lamv", [64, 4])
        prod = st.sb("prod", [64, 2])
        lexp = st.sb("lexp", [P, 2])
        sink_row = st.sb("sink_row", [1, 8])
        tps = st.ps("tps", [P, 4, P])
        vps = st.ps("vps", [P, 512])
        consts, loaded = st.sem("consts"), st.sem("loaded")
        cleared = st.sem("cleared")
        silu, turned, turned_v, copied = st.sem("silu"), st.sem("turned"), st.sem("turned_v"), st.sem("copied")
        lam_prod, lam_sum, lam_exp, lam_diff = st.sem("lam_prod"), st.sem("lam_sum"), st.sem("lam_exp"), st.sem("lam_diff")
        done = st.sem("done")
        fill = st.sb("fill", [P, 8 * HALF_ROWS * GRID_W * GRID_W // P])
        filled, padded, rpb_in = st.sem("filled"), st.sem("padded"), st.sem("rpb_in")
        block = st.block()
        nconv = DEPTH * 3 * 2 * KF
        conv_w = IN["ffn_conv_w"].rearrange("l j (t p) -> (l j t) p", p=P)
        conv_b = IN["ffn_conv_b"].rearrange("l (t p) -> (l t) p", p=P)
        small = [("a_q_norm", GV_AQ), ("a_k_norm", GV_AK), ("b_q_norm", GV_BQ), ("b_k_norm", GV_BK),
                 ("d_q_norm", GV_DQ), ("d_k_norm", GV_DK)]
        loads = []
        for n, c in small:
            for half in (0, 64):
                loads.append((G.GV[half:half + 64, c:c + 1], IN[n].rearrange("a d -> d a")))
        for n, c in (("c_q_norm", GV_CQ), ("c_k_norm", GV_CK)):
            loads.append((G.GV[0:C_DQK, c:c + 1], IN[n].rearrange("a d -> d a")))
        loads.append((G.GV[:, GV_SUB:GV_SUB + 1], IN["a_subln"].rearrange("a d -> d a")))
        for n, c, w in (("c_q_a_norm", GV_CQA, Q_LORA), ("c_kv_a_norm", GV_CKVA, KV_LORA)):
            for k in range(w // P):
                loads.append((G.GV[:, c + k:c + k + 1], IN[n][:, k * P:(k + 1) * P].rearrange("a d -> d a")))
        for i, n in enumerate(("a_lam_q1", "a_lam_k1", "a_lam_q2", "a_lam_k2")):
            loads.append((lamv[:, i:i + 1], IN[n].rearrange("a d -> d a")))
        loads.append((sink_row[:, :], IN["d_sink"]))
        loads.append((vec[0:8, :], IN["c"].rearrange("a (k p) -> (a k) p", p=P)))
        loads.append((vec[8:16, :], IN["c_ctx"].rearrange("(k p) -> k p", p=P)))
        loads.append((rows[0:16, 0, :], IN["norm_mix"].rearrange("l (k p) -> (l k) p", p=P)))
        loads.append((rows[16:32, 0, :], IN["norm_ffn"].rearrange("l (k p) -> (l k) p", p=P)))
        loads.append((rows[32:128, 0, :], IN["ada_b"].rearrange("l (k p) -> (l k) p", p=P)))
        loads.append((rows[:, 1, :], conv_w[0:128]))
        loads.append((rows[:, 2, :], conv_w[128:256]))
        loads.append((rows[0:8, 3, :], conv_w[256:nconv]))
        loads.append((rows[8:96, 3, :], conv_b))
        assert nconv == 264 and PRM_CONV_W == P

        @block.sync
        def _(sp):
            sp.dma_start(G.IDENT[:, :], IN["k_ident"]).then_inc(consts, 16)
            sp.dma_start(G.BLK64[:, :], IN["k_blk64"]).then_inc(consts, 16)
            sp.dma_start(G.ROT[:, :], IN["k_rot"]).then_inc(consts, 16)
            sp.dma_start(G.ROT96[:, :], IN["k_rot96"]).then_inc(consts, 16)
            sp.wait_ge(cleared, 1)
            for dst, src in loads:
                sp.dma_start(dst, src).then_inc(loaded, 16)
            sp.wait_ge(filled, 1)
            sp.dma_start(G.RPB.rearrange("h r c k -> (h r c k)").rearrange("(p n) -> p n", p=P), fill[:, :]).then_inc(padded, 16)
            sp.wait_ge(padded, 16)
            edge = NA_W // 2
            for h in range(8):
                dst = bass.AP(tensor=G.RPB.tensor, offset=h * HALF_ROWS * GRID_W * GRID_W + edge * GRID_W,
                              ap=[[GRID_W * GRID_W, HALF_ROWS], [GRID_W + 1, GRID_W - NA_W + 1], [1, NA_W]])
                src = bass.AP(tensor=IN["b_rpb"].tensor, offset=h * HALF_ROWS * HALF_COLS + NA_W - 1 - edge,
                              ap=[[HALF_COLS, HALF_ROWS], [0, GRID_W - NA_W + 1], [1, NA_W]])
                sp.dma_start(dst, src).then_inc(rpb_in, 16)
            edges = list(range(edge)) + list(range(GRID_W - edge + 1, GRID_W))
            for c in edges:
                k0 = 0 if c < edge else GRID_W - NA_W
                sp.dma_start(G.RPB[:, :, c, k0:k0 + NA_W],
                             IN["b_rpb"][0, :, :, k0 - c + NA_W - 1:k0 - c + 2 * NA_W - 1]).then_inc(rpb_in, 16)
            sp.wait_ge(rpb_in, 16 * (8 + len(edges)))

        @block.gpsimd
        def _(pool):
            pool.memset(G.GV[:, :], 0.0).then_inc(cleared, 1)
            pool.memset(G.ONES[:, :], 1.0).then_inc(done, 1)
            pool.memset(G.EPSC[:, :], EPS).then_inc(done, 1)
            pool.memset(fill[:, :], NEG).then_inc(filled, 1)

        @block.scalar
        def _(act):
            act.wait_ge(loaded, 16 * len(loads))
            act.activation(svec[:, :], vec[:, :], ACT.Silu).then_inc(silu, 1)
            act.wait_ge(lam_sum, 2)
            act.activation(lexp[:, :], vps[:, 32:34], ACT.Exp).then_inc(lam_exp, 1)

        @block.tensor
        def _(pe):
            pe.wait_ge(consts, 64)
            pe.wait_ge(loaded, 16 * len(loads))
            for g in range(4):
                n = P if g < 3 else 96
                t = pe.transpose(tps[:, g, 0:n], rows[0:n, g, :], G.IDENT[0:n, 0:n])
            t.then_inc(turned, 1)
            pe.wait_ge(silu, 1)
            pe.transpose(vps[:, 0:16], svec[:, :], G.IDENT[0:16, 0:16]).then_inc(turned_v, 1)
            pe.wait_ge(done, 2)
            pe.wait_ge(lam_prod, 1)
            pe.matmul(vps[:, 32:34], G.ONES[0:64, :], prod[:, :], start=True, stop=True).then_inc(lam_sum, 1)
            pe.matmul(vps[:, 64:72], G.ONES[0:1, :], sink_row[:, :], start=True, stop=True).then_inc(lam_sum, 1)

        @block.vector
        def _(dve):
            dve.wait_ge(loaded, 16 * len(loads))
            dve.wait_ge(consts, 64)
            dve.tensor_tensor(prod[:, :], lamv[:, 0:4:2], lamv[:, 1:4:2], ALU.mult).then_inc(lam_prod, 1)
            qcols = [GV_AQ, GV_BQ, GV_DQ]
            for i, c in enumerate(qcols):
                dve.tensor_scalar(G.GV[:, c:c + 1], G.GV[:, c:c + 1], 64 ** -0.5, None, ALU.mult).then_inc(copied, 1)
            dve.tensor_scalar(G.GV[:, GV_CQ:GV_CQ + 1], G.GV[:, GV_CQ:GV_CQ + 1], C_DQK ** -0.5, None,
                              ALU.mult).then_inc(copied, 1)
            dve.tensor_scalar(G.GV[:, GV_SUB:GV_SUB + 1], G.GV[:, GV_SUB:GV_SUB + 1], 1.0 - LAM_INIT, None,
                              ALU.mult).then_inc(copied, 1)
            dve.wait_ge(copied, 5)
            for i, c in enumerate((GV_AQ, GV_AK, GV_DQ, GV_DK)):
                dve.tensor_scalar(G.ROTG[:, i, :], G.ROT[:, :], G.GV[:, c:c + 1], None, ALU.mult).then_inc(copied, 1)
            for i, c in enumerate((GV_CQ, GV_CK)):
                dve.tensor_scalar(G.ROTG[0:C_DQK, 4 + i, 0:C_DQK], G.ROT96[:, :], G.GV[0:C_DQK, c:c + 1], None,
                                  ALU.mult).then_inc(copied, 1)
            dve.wait_ge(turned, 1)
            dve.tensor_copy(G.PRM[:, 0:384], tps[:, 0:3, :].rearrange("p a b -> p (a b)")).then_inc(copied, 1)
            dve.tensor_copy(G.PRM[:, 384:PRM_N], tps[:, 3, 0:96]).then_inc(copied, 1)
            dve.wait_ge(turned_v, 1)
            dve.wait_ge(lam_sum, 2)
            dve.wait_ge(lam_exp, 1)
            dve.tensor_copy(G.CVEC[:, :], vps[:, 0:16]).then_inc(copied, 1)
            dve.tensor_copy(G.SINK[:, :], vps[:, 64:72]).then_inc(copied, 1)
            dve.tensor_tensor(G.NLAM[:, :], lexp[:, 1:2], lexp[:, 0:1], ALU.subtract).then_inc(lam_diff, 1)
            dve.wait_ge(lam_diff, 1)
            dve.tensor_scalar(G.NLAM[:, :], G.NLAM[:, :], -LAM_INIT, None, ALU.add).then_inc(lam_diff, 1)
            dve.wait_ge(lam_diff, 2)
            dve.tensor_scalar(G.LINV[:, :], G.NLAM[:, :], -1.0, 1.0, ALU.mult, ALU.max).then_inc(lam_diff, 1)
            dve.wait_ge(lam_diff, 3)
            dve.tensor_tensor(G.LINV[:, :], G.LINV[:, :], G.NLAM[:, :], ALU.max).then_inc(lam_diff, 1)
            dve.wait_ge(lam_diff, 4)
            dve.reciprocal(G.LINV[:, :], G.LINV[:, :]).then_inc(lam_diff, 1)
            dve.wait_ge(lam_diff, 5)
            dve.tensor_tensor(G.NLAM[:, :], G.NLAM[:, :], G.LINV[:, :], ALU.mult).then_inc(copied, 1)
            dve.tensor_scalar(G.EPSL[:, :], G.LINV[:, :], G.LINV[:, 0:1], EPS, ALU.mult, ALU.mult).then_inc(copied, 1)


def transpose_in(nc, G, IN):
    with Stage(nc, "xin") as st:
        tok = st.sb("tok", [P, 2, D])
        xt = st.sb("xt", [P, 2, KD, P])
        tps = st.ps("tps", [P, 2, KD, P])
        load, turn, copy_a, copy_v, store = (st.sems(n) for n in ("load", "turn", "copy_a", "copy_v", "store"))
        block = st.block()
        X = IN["x"].rearrange("a (t p) d -> (a t) p d", p=P)
        C = IN["ctx"].rearrange("a (t p) d -> (a t) p d", p=P)
        XT = G.X.rearrange("(k p) t -> p k t", p=P)
        jobs = [(C, CTX // P, 0), (X, LAT // P, CTX)]

        @block.sync
        def _(sp):
            used = [0, 0]
            for src, n, t0 in jobs:
                for its in sweep(sp, n, used):
                    for m, s, u, it, other in its:
                        sp.wait_ge(turn[s], u)
                        sp.dma_start(tok[:, s, :], src[bass.ds(m, 1)].rearrange("a p d -> (a p) d")).then_inc(load[s], 16)

        @block.tensor
        def _(pe):
            used = [0, 0]
            for src, n, t0 in jobs:
                for its in sweep(pe, n, used):
                    for m, s, u, it, other in its:
                        pe.wait_ge(load[s], 16 * u + 16)
                        pe.wait_ge(copy_a[s], u)
                        pe.wait_ge(copy_v[s], u)
                        for k in range(KD):
                            t = pe.transpose(tps[:, s, k, :], tok[:, s, k * P:(k + 1) * P], G.IDENT[:, :])
                        t.then_inc(turn[s], 1)

        @block.scalar
        def _(act):
            used = [0, 0]
            for src, n, t0 in jobs:
                for its in sweep(act, n, used):
                    for m, s, u, it, other in its:
                        act.wait_ge(turn[s], u + 1)
                        act.wait_ge(store[s], 16 * u)
                        act.activation(xt[:, s, 0:4, :], tps[:, s, 0:4, :], ACT.Copy).then_inc(copy_a[s], 1)
                        act.wait_ge(copy_a[s], u + 1)
                        act.wait_ge(copy_v[s], u + 1)
                        act.dma_start(XT[:, :, bass.ds(t0 + m * P, P)], xt[:, s, :, :]).then_inc(store[s], 16)
            for s in range(2):
                act.wait_ge(store[s], 16 * used[s])

        @block.vector
        def _(dve):
            used = [0, 0]
            for src, n, t0 in jobs:
                for its in sweep(dve, n, used):
                    for m, s, u, it, other in its:
                        dve.wait_ge(turn[s], u + 1)
                        dve.wait_ge(store[s], 16 * u)
                        dve.tensor_copy(xt[:, s, 4:8, :], tps[:, s, 4:8, :]).then_inc(copy_v[s], 1)


def modulation(nc, G, IN):
    with Stage(nc, "ada") as st:
        w = st.sb("w", [P, 2, KD, 512])
        row = st.sb("row", [2, DEPTH, 6 * D])
        mps = st.ps("mps", [2, 2, 512])
        cps = st.ps("cps", [P, DEPTH, 512])
        load, mult, copy = (st.sems(n) for n in ("load", "mult", "copy"))
        turned, added, scaled = st.sem("turned"), st.sem("added"), st.sem("scaled")
        block = st.block()
        n = 6 * D // 512
        cvec = G.CVEC[:, :].rearrange("p (v k) -> p k v", v=2)

        @block.sync
        def _(sp):
            used = [0, 0]
            for layer in range(DEPTH):
                W = IN["ada_w"][layer].rearrange("(k p) n -> p k n", p=P)
                for its in sweep(sp, n, used):
                    for m, s, u, it, other in its:
                        sp.wait_ge(mult[s], u)
                        sp.dma_start(w[:, s, :, :], W[:, :, bass.ds(m * 512, 512)]).then_inc(load[s], 16)

        @block.tensor
        def _(pe):
            used = [0, 0]
            for layer in range(DEPTH):
                for its in sweep(pe, n, used):
                    for m, s, u, it, other in its:
                        pe.wait_ge(load[s], 16 * u + 16)
                        pe.wait_ge(copy[s], u)
                        for k in range(KD):
                            t = pe.matmul(mps[:, s, :], cvec[:, k, :], w[:, s, k, :], start=(k == 0), stop=(k == KD - 1))
                        t.then_inc(mult[s], 1)
            for s in range(2):
                pe.wait_ge(copy[s], used[s])
            for layer in range(DEPTH):
                for j in range(6 * KD):
                    t = pe.transpose(cps[:, layer, 2 * j:2 * j + 2], row[:, layer, j * P:(j + 1) * P], G.IDENT[0:2, 0:2])
                t.then_inc(turned, 1)

        @block.scalar
        def _(act):
            used = [0, 0]
            for layer in range(DEPTH):
                for its in sweep(act, n, used):
                    for m, s, u, it, other in its:
                        act.wait_ge(mult[s], u + 1)
                        act.activation(row[:, layer, bass.ds(m * 512, 512)], mps[:, s, :], ACT.Copy).then_inc(copy[s], 1)

        @block.vector
        def _(dve):
            for layer in range(DEPTH):
                dve.wait_ge(turned, layer + 1)
                bias = G.PRM[:, PRM_ADA_B + layer * 48:PRM_ADA_B + layer * 48 + 48]
                mod = G.MOD[:, layer, :, :]
                cols = cps[:, layer, 0:12 * KD].rearrange("p (j v) -> p j v", v=2)
                for v in range(2):
                    dve.tensor_tensor(mod[:, :, v], cols[:, :, v], bias, ALU.add).then_inc(added, 1)
                dve.wait_ge(added, 2 * layer + 2)
                for which, norm, part in ((0, PRM_NORM_MIX, 1), (1, PRM_NORM_FFN, 4)):
                    g = G.PRM[:, norm + layer * KD:norm + layer * KD + KD]
                    for v in range(2):
                        dve.scalar_tensor_tensor(out=G.GS[:, layer, which, :, v], in0=mod[:, part * KD:part * KD + KD, v],
                                                 scalar=1.0, in1=g, op0=ALU.add, op1=ALU.mult).then_inc(scaled, 1)


class Operand:

    def __init__(self, G, src, kt, t0, t1, act_h, act_l, scale=None, shift=None, norm=True, mean_over=D, sub_tiles=0):
        self.G, self.src, self.kt, self.t0, self.t1 = G, src, kt, t0, t1
        self.act_h, self.act_l, self.scale, self.shift = act_h, act_l, scale, shift
        self.norm, self.mean_over = norm, mean_over
        self.nsq = kt if norm else sub_tiles

    def allocate(self, st, acc, spare=()):
        T = self.t1 - self.t0
        self.acc = acc
        own = max(1, self.kt - 2 * len(spare)) if self.kt > 4 else self.kt
        xs = st.sb("op_x", [P, own, T])
        self.tiles = [(xs, k) for k in range(own)] + [(b, s) for b in spare for s in range(2)]
        if self.nsq:
            self.sq = st.sb("op_sq", [P, 2, T])
            self.rs = st.sb("op_rs", [P, 1 if self.norm else self.nsq, T])
        self.loaded = st.sems("x_loaded", self.kt)
        self.squared, self.summed, self.logged, self.rstd = (
            st.sem(n) for n in ("op_squared", "op_summed", "op_logged", "op_rstd"))
        self.normed, self.modded, self.hi, self.lo = (st.sem(n) for n in ("op_normed", "op_modded", "op_hi", "op_lo"))

    def x(self, k, a=0, b=None):
        buffer, slot = self.tiles[k]
        return buffer[:, slot, a:self.t1 - self.t0 if b is None else b]

    def load(self, sp):
        S = self.src.rearrange("(k p) t -> k p t", p=P)
        for k in range(self.kt):
            sp.dma_start(self.x(k), S[k, :, self.t0:self.t1]).then_inc(self.loaded[k], 16)

    def sum_squares(self, pe):
        for k in range(self.nsq):
            pe.wait_ge(self.squared, k + 1)
            if not self.norm and k >= 2:
                pe.wait_ge(self.logged, k - 1)
            for a, b in chunks(0, self.t1 - self.t0):
                t = pe.matmul(self.acc[:, 0 if self.norm else k % 2, a:b], self.G.ONES[:, :], self.sq[:, k % 2, a:b],
                              start=(k == 0 or not self.norm), stop=(k == self.kt - 1 or not self.norm))
            t.then_inc(self.summed, 1)

    def scale_and_round(self, act):
        G, T, t0, norm, kt = self.G, self.t1 - self.t0, self.t0, self.norm, self.kt
        for k in range(self.nsq):
            act.wait_ge(self.loaded[k], 16)
            if k >= 2:
                act.wait_ge(self.summed, k - 1)
            act.activation(self.sq[:, k % 2, :], self.x(k), ACT.Square).then_inc(self.squared, 1)
            if not norm:
                act.wait_ge(self.summed, k + 1)
                act.activation(self.rs[:, k, :], self.acc[:, k % 2, 0:T], ACT.Sqrt, scale=1.0 / self.mean_over,
                               bias=G.EPSL[:, 0:1]).then_inc(self.logged, 1)
        if norm:
            act.wait_ge(self.summed, kt)
            act.activation(self.rs[:, 0, :], self.acc[:, 0, 0:T], ACT.Ln, scale=1.0 / self.mean_over,
                           bias=G.EPSC[:, 0:1]).then_inc(self.logged, 1)
            act.wait_ge(self.logged, 1)
            act.activation(self.rs[:, 0, :], self.rs[:, 0, :], ACT.Exp, scale=-0.5).then_inc(self.rstd, 1)
        modded = 0
        for k in range(kt):
            if k < self.nsq:
                act.wait_ge(self.normed, k + 1)
            act.wait_ge(self.loaded[k], 16)
            pieces = self.scale(k) if self.scale else []
            for i, (column, a, b) in enumerate(pieces):
                x = self.x(k, a - t0, b - t0)
                if self.shift:
                    t = act.activation(x, x, ACT.Identity, scale=column, bias=self.shift(k)[i][0])
                else:
                    t = act.activation(x, x, ACT.Identity, scale=column)
                t.then_inc(self.modded, 1)
            if pieces:
                modded += len(pieces)
                act.wait_ge(self.modded, modded)
            act.activation(self.act_h[:, k, 0:T], self.x(k), ACT.Copy).then_inc(self.hi, 1)

    def norm_and_rest(self, dve):
        T, norm, kt = self.t1 - self.t0, self.norm, self.kt
        for k in range(kt + 1):
            if k < self.nsq:
                if not norm:
                    dve.wait_ge(self.logged, k + 1)
                    dve.reciprocal(self.rs[:, k, :], self.rs[:, k, :]).then_inc(self.rstd, 1)
                dve.wait_ge(self.rstd, 1 if norm else k + 1)
                dve.tensor_tensor(self.x(k), self.x(k), self.rs[:, 0 if norm else k, :], ALU.mult).then_inc(self.normed, 1)
            if k >= 1:
                dve.wait_ge(self.hi, k)
                dve.tensor_tensor(self.act_l[:, k - 1, 0:T], self.x(k - 1), self.act_h[:, k - 1, 0:T].bitcast(F32),
                                  ALU.subtract).then_inc(self.lo, 1)


class Weights:

    def __init__(self, st, kt):
        self.kt = kt
        self.raw = st.sb("w_raw", [P, 2, kt, P])
        self.hi = st.sb("w_hi", [P, 2, kt, P], F32R)
        self.lo = st.sb("w_lo", [P, 2, kt, P], F32R)
        self.loaded, self.hi_ready, self.lo_ready = st.sems("w_loaded"), st.sems("w_hi_ready"), st.sems("w_lo_ready")
        self.multiplied = st.sems("multiplied")


def load_weights(sp, W, wd, segs):
    V = wd.rearrange("(k p) m -> p k m", p=P)
    used = [0, 0]
    for g in segs:
        for its in sweep(sp, g["tiles"], used):
            for m, s, u, it, other in its:
                sp.wait_ge(W.lo_ready[s], u)
                sp.dma_start(W.raw[:, s, :, 0:g["mw"]], V[:, :, bass.ds(g["col"](m, s, it), g["mw"])])\
                  .then_inc(W.loaded[s], 16)


def split_weights(pool, W, segs, ones):
    used = [0, 0]
    for g in segs:
        mw = g["mw"]
        for its in sweep(pool, g["tiles"], used):
            for m, s, u, it, other in its:
                pool.wait_ge(W.loaded[s], 16 * u + 16)
                pool.wait_ge(W.multiplied[s], u)
                pool.tensor_tensor(W.hi[:, s, :, 0:mw], W.raw[:, s, :, 0:mw],
                                   ones[:, 0:mw].unsqueeze(1).broadcast_to([P, W.kt, mw]), ALU.mult)\
                    .then_inc(W.hi_ready[s], 1)
                pool.wait_ge(W.hi_ready[s], u + 1)
                pool.tensor_tensor(W.lo[:, s, :, 0:mw], W.raw[:, s, :, 0:mw], W.hi[:, s, :, 0:mw].bitcast(F32),
                                   ALU.subtract).then_inc(W.lo_ready[s], 1)


def multiply(pe, W, act_h, act_l, acc, g, a0, s, u, op=None, between=None, jobs=0):
    mw = g["mw"]
    t0, t1 = g["toks"]
    pe.wait_ge(W.lo_ready[s], u + 1)
    first = op is not None and s == 0 and isinstance(u, int) and u == 0
    cs = chunks(t0, t1)
    steps = [(k, c) for k in range(W.kt) for c in cs] if first else [(k, c) for c in cs for k in range(W.kt)]
    done = 0
    for i, (k, (a, b)) in enumerate(steps):
        if first and (a, b) == cs[0]:
            pe.wait_ge(op.lo, k + 1)
        for w, x in ((W.hi, act_h), (W.hi, act_l), (W.lo, act_h)):
            t = pe.matmul(acc[0:mw, s, a - t0:b - t0], w[:, s, k, 0:mw], x[:, k, a - a0:b - a0],
                          start=(k == 0 and w is W.hi and x is act_h), stop=(k == W.kt - 1 and w is W.lo))
        if i == len(steps) - 1:
            t.then_inc(W.multiplied[s], 1)
        while done < jobs and (i == len(steps) - 1 or done * len(steps) < 2 * jobs * (i + 1 - len(steps) // 4)):
            between(done)
            done += 1


def project_store(nc, G, name, wd, kt, act_h, act_l, a0, segs, out, op=None):
    with Stage(nc, name) as st:
        W = Weights(st, kt)
        ob = st.sb("ob", [P, 2, NT])
        acc = st.ps("acc", [P, 2, 1536])
        ev_a, ev_v, stored = (st.sems(n) for n in ("ev_a", "ev_v", "stored"))
        if op:
            op.allocate(st, acc)
        block = st.block()

        @block.sync
        def _(sp):
            if op:
                op.load(sp)
            load_weights(sp, W, wd, segs)

        @block.gpsimd
        def _(pool):
            split_weights(pool, W, segs, G.ONES)

        @block.tensor
        def _(pe):
            if op:
                op.sum_squares(pe)
            used = [0, 0]
            for g in segs:
                for its in sweep(pe, g["tiles"], used):
                    for m, s, u, it, other in its:
                        pe.wait_ge(ev_a[s], u)
                        pe.wait_ge(ev_v[s], u)
                        multiply(pe, W, act_h, act_l, acc, g, a0, s, u, op)

        @block.scalar
        def _(act):
            if op:
                op.scale_and_round(act)
            used = [0, 0]
            for g in segs:
                T, mw = g["toks"][1] - g["toks"][0], g["mw"]
                for its in sweep(act, g["tiles"], used):
                    for m, s, u, it, other in its:
                        act.wait_ge(W.multiplied[s], u + 1)
                        act.wait_ge(stored[s], 16 * u)
                        act.activation(ob[0:mw, s, 0:512], acc[0:mw, s, 0:512], ACT.Copy).then_inc(ev_a[s], 1)
                        act.wait_ge(ev_a[s], u + 1)
                        act.wait_ge(ev_v[s], u + 1)
                        act.dma_start(out[bass.ds(g["row"] + m * mw, mw), g["toks"][0]:g["toks"][1]],
                                      ob[0:mw, s, 0:T]).then_inc(stored[s], 16)
            for s in range(2):
                act.wait_ge(stored[s], 16 * used[s])

        @block.vector
        def _(dve):
            if op:
                op.norm_and_rest(dve)
            used = [0, 0]
            for g in segs:
                T, mw = g["toks"][1] - g["toks"][0], g["mw"]
                for its in sweep(dve, g["tiles"], used):
                    for m, s, u, it, other in its:
                        dve.wait_ge(W.multiplied[s], u + 1)
                        dve.wait_ge(stored[s], 16 * u)
                        dve.tensor_copy(ob[0:mw, s, 512:T], acc[0:mw, s, 512:T]).then_inc(ev_v[s], 1)


def project_heads(nc, G, name, wd, kt, act_h, act_l, a0, segs, out, tables=None, kr=None, v_out=None, op=None):
    with Stage(nc, name) as st:
        W = Weights(st, kt)
        cos, sin = st.sb("cos", [P, NT]), st.sb("sin", [P, NT])
        raw, sq, ob = st.sb("raw", [P, 2, NT]), st.sb("sq", [P, 2, NT]), st.sb("ob", [P, 2, NT])
        rs, rot = st.sb("rs", [P, NT]), st.sb("rot", [P, NT])
        vb = st.sb("vb", [P, 2, NT]) if v_out is not None else None
        acc, aux = st.ps("acc", [P, 2, 1536]), st.ps("aux", [P, 2, 512])
        tab, kr_in = st.sem("tab"), st.sem("kr_in")
        raw_ready, sq_ready, v_ready, normed, stored, v_stored = (
            st.sems(n) for n in ("raw_ready", "sq_ready", "v_ready", "normed", "stored", "v_stored"))
        aux_ready, aux_free = st.sems("aux_ready"), st.sems("aux_free")
        rstd, with_cos, with_rot = st.sem("rstd"), st.sem("with_cos"), st.sem("with_rot")
        if op:
            op.allocate(st, acc, (raw, ob))
        block = st.block()

        def parts(g):
            T = g["toks"][1] - g["toks"][0]
            return chunks(0, T, T // 4 if T > 1024 else 512)

        def jobs(g):
            return len(parts(g)) * (2 if g["rope"] is not None else 1)

        def walk(eng, body):
            used, sums, before = [0, 0], (0, 0, 0), None
            for g in segs:
                for its in sweep(eng, g["tiles"], used, lag=True):
                    if not isinstance(its[0][0], int):
                        m, s, u, it, other = its[1]
                        before = (g, m - 2, s, u - 1, other - 1) + sums
                    for m, s, u, it, other in its:
                        body((g, m, s, u, other) + sums, before)
                        before = (g, m, s, u, other) + sums
                s = 1 - g["tiles"] % 2
                before = (g, g["tiles"] - 1, s, used[s] - 1, used[1 - s]) + sums
                sums = (sums[0] + g["tiles"] * jobs(g) // 2, sums[1] + g["tiles"],
                        sums[2] + (g["tiles"] if g["rope"] is not None else 0))
            body(None, before)
            return used

        @block.sync
        def _(sp):
            if op:
                op.load(sp)
            if tables is not None:
                nr = tables[0].shape[0]
                sp.dma_start(cos[0:nr, :], tables[0]).then_inc(tab, 16)
                sp.dma_start(sin[0:nr, :], tables[1]).then_inc(tab, 16)
            if kr is not None:
                for s in range(2):
                    sp.dma_start(raw[64:C_DQK, s, :], kr).then_inc(kr_in, 16)
            load_weights(sp, W, wd, segs)

        @block.gpsimd
        def _(pool):
            split_weights(pool, W, segs, G.ONES)

        @block.tensor
        def _(pe):
            if op:
                op.sum_squares(pe)
            def sum_and_turn(tile, j):
                g, m, s, u, other, bank_uses, tiles, ropes = tile
                rows, ps = g["rows"], parts(g)
                if j == 0:
                    pe.wait_ge(sq_ready[s], u + 1)
                    pe.wait_ge(raw_ready[s], u + 1)
                mat, x = (g["ones"], sq) if j < len(ps) else (g["rope"], raw)
                a, b = ps[j % len(ps)]
                pe.wait_ge(aux_free[j % 2], bank_uses + m * (jobs(g) // 2) + j // 2)
                pe.matmul(aux[0:rows, j % 2, 0:b - a], mat[0:rows, 0:rows], x[0:rows, s, a:b], start=True,
                          stop=True).then_inc(aux_ready[j % 2], 1)

            def body(tile, before):
                n = jobs(before[0]) if before is not None else 0
                if tile is None:
                    for j in range(n):
                        sum_and_turn(before, j)
                    return
                g, m, s, u = tile[:4]
                pe.wait_ge(raw_ready[s], u)
                if v_out is not None:
                    pe.wait_ge(v_ready[s], u)
                multiply(pe, W, act_h, act_l, acc, g, a0, s, u, op, lambda j: sum_and_turn(before, j), n)
            walk(pe, body)

        @block.scalar
        def _(act):
            if op:
                op.scale_and_round(act)
            if kr is not None:
                act.wait_ge(kr_in, 32)

            def store(tile):
                g, m, s, u = tile[:4]
                rows = g["rows"]
                act.wait_ge(normed[s], u + 1)
                act.dma_start(out[bass.ds(g["row"] + m * rows, rows), g["toks"][0]:g["toks"][1]],
                              ob[0:rows, s, 0:g["toks"][1] - g["toks"][0]]).then_inc(stored[s], 16)

            def body(tile, before):
                if before is not None:
                    g, m, s, u, other, bank_uses, tiles, ropes = before
                    T, rows, n = g["toks"][1] - g["toks"][0], g["rows"], jobs(g)
                    act.wait_ge(normed[s], u)
                    act.wait_ge(normed[1 - s], other)
                    for j, (a, b) in enumerate(parts(g)):
                        act.wait_ge(aux_ready[j % 2], bank_uses + m * (n // 2) + j // 2 + 1)
                        act.activation(rs[0:rows, a:b], aux[0:rows, j % 2, 0:b - a], ACT.Ln, scale=1.0 / g["width"],
                                       bias=G.EPSC[0:rows, 0:1]).then_inc(aux_free[j % 2], 1)
                    for b in range(2):
                        act.wait_ge(aux_free[b], bank_uses + m * (n // 2) + len(parts(g)) // 2)
                    act.activation(rs[0:rows, 0:T], rs[0:rows, 0:T], ACT.Exp, scale=-0.5).then_inc(rstd, 1)
                if tile is not None:
                    g, m, s, u = tile[:4]
                    T, rows, own = g["toks"][1] - g["toks"][0], g["rows"], g["own"]
                    act.wait_ge(W.multiplied[s], u + 1)
                    act.wait_ge(normed[s], u)
                    act.activation(raw[0:own, s, 0:T], acc[0:own, s, 0:T], ACT.Copy).then_inc(raw_ready[s], 1)
                    if v_out is not None:
                        act.wait_ge(v_stored[s], 16 * u)
                        act.activation(vb[64:P, s, 0:T], acc[64:P, s, 0:T], ACT.Copy).then_inc(v_ready[s], 1)
                    act.wait_ge(raw_ready[s], u + 1)
                    act.activation(sq[0:rows, s, 0:T], raw[0:rows, s, 0:T], ACT.Square).then_inc(sq_ready[s], 1)
                    if v_out is not None:
                        act.wait_ge(v_ready[s], u + 1)
                        act.dma_start(v_out[bass.ds(m * 64, 64), :], vb[64:P, s, 0:T]).then_inc(v_stored[s], 16)
                if before is not None:
                    store(before)

            used = walk(act, body)
            for s in range(2):
                act.wait_ge(stored[s], 16 * used[s])
                if v_out is not None:
                    act.wait_ge(v_stored[s], 16 * used[s])

        @block.vector
        def _(dve):
            if op:
                op.norm_and_rest(dve)
            if tables is not None:
                dve.wait_ge(tab, 32)

            def body(tile, before):
                if tile is None:
                    return
                g, m, s, u, other, bank_uses, tiles, ropes = tile
                (t0, t1), rows, n = g["toks"], g["rows"], jobs(g)
                T = t1 - t0
                gain = G.GV[0:rows, g["gain"]:g["gain"] + 1]
                dve.wait_ge(raw_ready[s], u + 1)
                dve.wait_ge(stored[s], 16 * u)
                x, o = raw[0:rows, s, 0:T], ob[0:rows, s, 0:T]
                if g["rope"] is None:
                    dve.wait_ge(rstd, tiles + m + 1)
                    dve.scalar_tensor_tensor(out=o, in0=x, scalar=gain, in1=rs[0:rows, 0:T], op0=ALU.mult,
                                             op1=ALU.mult).then_inc(normed[s], 1)
                    return
                dve.scalar_tensor_tensor(out=o, in0=x, scalar=gain, in1=cos[0:rows, t0:t1], op0=ALU.mult,
                                         op1=ALU.mult).then_inc(with_cos, 1)
                ps = parts(g)
                for i, (a, b) in enumerate(ps):
                    j = len(ps) + i
                    dve.wait_ge(aux_ready[j % 2], bank_uses + m * (n // 2) + j // 2 + 1)
                    dve.tensor_tensor(rot[0:rows, a:b], aux[0:rows, j % 2, 0:b - a], sin[0:rows, t0 + a:t0 + b],
                                      ALU.mult).then_inc(aux_free[j % 2], 1)
                dve.wait_ge(with_cos, ropes + m + 1)
                for b in range(2):
                    dve.wait_ge(aux_free[b], bank_uses + (m + 1) * (n // 2))
                dve.tensor_tensor(o, o, rot[0:rows, 0:T], ALU.add).then_inc(with_rot, 1)
                dve.wait_ge(with_rot, ropes + m + 1)
                dve.wait_ge(rstd, tiles + m + 1)
                dve.tensor_tensor(o, o, rs[0:rows, 0:T], ALU.mult).then_inc(normed[s], 1)
            walk(dve, body)


def project_residual(nc, G, name, wd, kt, act_h, act_l, a0, layer, toks, part, op=None):
    t0, t1 = toks
    T = t1 - t0
    segs = [dict(tiles=KD, mw=P, col=lambda m, s, it: m * P, toks=toks)]
    with Stage(nc, name) as st:
        W = Weights(st, kt)
        x = st.sb("x", [P, 2, T])
        acc = st.ps("acc", [P, 2, 1536])
        x_in, added, stored = (st.sems(n) for n in ("x_in", "added", "stored"))
        if op:
            op.allocate(st, acc)
        block = st.block()
        ranges = [(v, max(a, t0), b) for v, a, b in ((1, 0, CTX), (0, CTX, NT)) if b > t0]

        @block.sync
        def _(sp):
            if op:
                op.load(sp)
            load_weights(sp, W, wd, segs)

        @block.gpsimd
        def _(pool):
            split_weights(pool, W, segs, G.ONES)

        @block.tensor
        def _(pe):
            if op:
                op.sum_squares(pe)
            for its in sweep(pe, KD, [0, 0]):
                for m, s, u, it, other in its:
                    pe.wait_ge(added[s], len(ranges) * u)
                    multiply(pe, W, act_h, act_l, acc, segs[0], a0, s, u, op)

        @block.scalar
        def _(act):
            if op:
                op.scale_and_round(act)
            used = [0, 0]
            for its in sweep(act, KD, used):
                for m, s, u, it, other in its:
                    act.wait_ge(stored[s], 16 * u)
                    act.dma_start(x[:, s, :], G.X[bass.ds(m * P, P), t0:t1]).then_inc(x_in[s], 16)
                for m, s, u, it, other in its:
                    act.wait_ge(added[s], len(ranges) * (u + 1))
                    act.dma_start(G.X[bass.ds(m * P, P), t0:t1], x[:, s, :]).then_inc(stored[s], 16)
            for s in range(2):
                act.wait_ge(stored[s], 16 * used[s])

        @block.vector
        def _(dve):
            if op:
                op.norm_and_rest(dve)
            for its in sweep(dve, KD, [0, 0]):
                for m, s, u, it, other in its:
                    dve.wait_ge(x_in[s], 16 * u + 16)
                    dve.wait_ge(W.multiplied[s], u + 1)
                    for v, a, b in ranges:
                        gate = G.MOD[:, layer, bass.ds(part * KD + m, 1), v]
                        dve.scalar_tensor_tensor(out=x[:, s, a - t0:b - t0], in0=acc[:, s, a - t0:b - t0], scalar=gate,
                                                 in1=x[:, s, a - t0:b - t0], op0=ALU.mult, op1=ALU.add)\
                           .then_inc(added[s], 1)


def ffn_up(nc, G, name, wd, act_h, act_l, a0, layer, toks, out, op=None):
    t0, t1 = toks
    T = t1 - t0
    segs = [dict(tiles=2 * KF, mw=P, col=lambda m, s, it: (it + s * KF) * P, toks=toks)]
    seqs = [(max(a, t0) - t0, b - t0) for a, b in ((0, CTX), (CTX, NT)) if b > t0]
    nseq = len(seqs)
    with Stage(nc, name) as st:
        W = Weights(st, KD)
        u_ = st.sb("conv", [P, 2, T])
        sg = st.sb("sg", [P, T])
        acc = st.ps("acc", [P, 2, 1536])
        mid, left, right = st.sems("mid"), st.sems("left"), st.sems("right")
        silu, gated, stored = st.sem("silu"), st.sem("gated"), st.sem("stored")
        if op:
            op.allocate(st, acc)
        block = st.block()

        def tap(j, s, it):
            return G.PRM[:, bass.ds(PRM_CONV_W + (layer * 3 + j) * 2 * KF + s * KF + it, 1)]

        @block.sync
        def _(sp):
            if op:
                op.load(sp)
            load_weights(sp, W, wd, segs)

        @block.gpsimd
        def _(pool):
            split_weights(pool, W, segs, G.ONES)

        @block.tensor
        def _(pe):
            if op:
                op.sum_squares(pe)
            for its in sweep(pe, 2 * KF, [0, 0]):
                for m, s, u, it, other in its:
                    pe.wait_ge(mid[s], u)
                    pe.wait_ge(right[s], nseq * u)
                    multiply(pe, W, act_h, act_l, acc, segs[0], a0, s, u, op)

        @block.scalar
        def _(act):
            if op:
                op.scale_and_round(act)
            for its in sweep(act, 2 * KF, [0, 0]):
                for m, s, u, it, other in its:
                    act.wait_ge(W.multiplied[s], u + 1)
                    act.wait_ge(gated, u)
                    if s == 1:
                        act.wait_ge(silu, u)
                    bias = G.PRM[:, bass.ds(PRM_CONV_B + layer * 2 * KF + s * KF + it, 1)]
                    act.activation(u_[:, s, :], acc[:, s, 0:T], ACT.Identity, scale=tap(1, s, it), bias=bias)\
                       .then_inc(mid[s], 1)
                act.wait_ge(right[1], nseq * (its[1][2] + 1))
                act.activation(sg[:, :], u_[:, 1, :], ACT.Silu).then_inc(silu, 1)
                act.wait_ge(gated, its[1][2] + 1)
                act.dma_start(out[bass.ds(it * P, P), t0:t1], u_[:, 0, :]).then_inc(stored, 16)
                act.wait_ge(stored, 16 * (its[1][2] + 1))

        @block.vector
        def _(dve):
            if op:
                op.norm_and_rest(dve)
            for its in sweep(dve, 2 * KF, [0, 0]):
                for m, s, u, it, other in its:
                    dve.wait_ge(mid[s], u + 1)
                    for a, b in seqs:
                        dve.scalar_tensor_tensor(out=u_[:, s, a + 1:b], in0=acc[:, s, a:b - 1], scalar=tap(0, s, it),
                                                 in1=u_[:, s, a + 1:b], op0=ALU.mult, op1=ALU.add).then_inc(left[s], 1)
                    dve.wait_ge(left[s], nseq * (u + 1))
                    for a, b in seqs:
                        dve.scalar_tensor_tensor(out=u_[:, s, a:b - 1], in0=acc[:, s, a + 1:b], scalar=tap(2, s, it),
                                                 in1=u_[:, s, a:b - 1], op0=ALU.mult, op1=ALU.add).then_inc(right[s], 1)
                u = its[1][2]
                dve.wait_ge(silu, u + 1)
                dve.wait_ge(right[0], nseq * (u + 1))
                dve.tensor_tensor(u_[:, 0, :], u_[:, 0, :], sg[:, :], ALU.mult).then_inc(gated, 1)


def ffn_down(nc, G, name, wd, hid, layer, ranges):
    with Stage(nc, name) as st:
        w_raw = st.sb("w_raw", [P, 2, D])
        w_hi, w_lo = st.sb("w_hi", [P, 2, D], F32R), st.sb("w_lo", [P, 2, D], F32R)
        h_raw = st.sb("h_raw", [P, 2, 512])
        h_hi, h_lo = st.sb("h_hi", [P, 2, 512], F32R), st.sb("h_lo", [P, 2, 512], F32R)
        x = st.sb("x", [P, 2, KD, 512])
        acc = st.ps("acc", [P, KD, 512])
        w_in, h_in, w_hi_ready, w_lo_ready, h_hi_ready, h_lo_ready, multiplied = (
            st.sems(n) for n in ("w_in", "h_in", "w_hi_ready", "w_lo_ready", "h_hi_ready", "h_lo_ready", "multiplied"))
        w2_lo_ready = st.sems("w2_lo_ready")
        x_in, summed, added, stored = st.sem("x_in"), st.sem("summed"), st.sem("added"), st.sem("stored")
        block = st.block()
        X = G.X.rearrange("(k p) t -> p k t", p=P)

        @block.sync
        def _(sp):
            def store(r):
                t0, t1 = ranges[r]
                for m in range(KD):
                    sp.wait_ge(added, KD * r + m + 1)
                    sp.dma_start(X[:, m, t0:t1], x[:, r % 2, m, 0:t1 - t0]).then_inc(stored, 16)

            used = [0, 0]
            for r, (t0, t1) in enumerate(ranges):
                T = t1 - t0
                for i, its in enumerate(sweep(sp, KF, used, lag=True)):
                    for k, s, u, it, other in its:
                        sp.wait_ge(w_lo_ready[s], u)
                        sp.wait_ge(w2_lo_ready[s], u)
                        sp.dma_start(w_raw[:, s, :], wd[bass.ds(k * P, P), :]).then_inc(w_in[s], 16)
                        sp.wait_ge(h_lo_ready[s], u)
                        sp.dma_start(h_raw[:, s, 0:T], hid[bass.ds(k * P, P), t0:t1]).then_inc(h_in[s], 16)
                    if i == 0:
                        if r >= 1:
                            store(r - 1)
                        if r >= 2:
                            sp.wait_ge(stored, 16 * KD * (r - 1))
                        sp.dma_start(x[:, r % 2, :, 0:T], X[:, :, t0:t1]).then_inc(x_in, 16)
            store(len(ranges) - 1)
            sp.wait_ge(stored, 16 * KD * len(ranges))

        @block.gpsimd
        def _(pool):
            used = [0, 0]
            for r in range(len(ranges)):
                for its in sweep(pool, KF, used, lag=True):
                    for k, s, u, it, other in its:
                        pool.wait_ge(w_in[s], 16 * u + 16)
                        pool.wait_ge(w_hi_ready[s], u + 1)
                        pool.wait_ge(multiplied[s], u)
                        pool.tensor_tensor(w_lo[:, s, 0:512], w_raw[:, s, 0:512], w_hi[:, s, 0:512].bitcast(F32),
                                           ALU.subtract).then_inc(w_lo_ready[s], 1)

        @block.scalar
        def _(act):
            used = [0, 0]
            for t0, t1 in ranges:
                T = t1 - t0
                for its in sweep(act, KF, used, lag=True):
                    for k, s, u, it, other in its:
                        act.wait_ge(multiplied[s], u)
                        act.wait_ge(w_in[s], 16 * u + 16)
                        act.activation(w_hi[:, s, :], w_raw[:, s, :], ACT.Copy).then_inc(w_hi_ready[s], 1)
                        act.wait_ge(h_in[s], 16 * u + 16)
                        act.activation(h_hi[:, s, 0:T], h_raw[:, s, 0:T], ACT.Copy).then_inc(h_hi_ready[s], 1)

        @block.tensor
        def _(pe):
            def step(r, s, u, first, last):
                T = ranges[r][1] - ranges[r][0]
                pe.wait_ge(w_lo_ready[s], u + 1)
                pe.wait_ge(w2_lo_ready[s], u + 1)
                pe.wait_ge(h_lo_ready[s], u + 1)
                for m in range(KD):
                    if first and r >= 1:
                        pe.wait_ge(added, KD * (r - 1) + m + 1)
                    for w, h in ((w_hi, h_hi), (w_hi, h_lo), (w_lo, h_hi)):
                        t = pe.matmul(acc[:, m, 0:T], w[:, s, m * P:(m + 1) * P], h[:, s, 0:T],
                                      start=first and w is w_hi and h is h_hi, stop=last and w is w_lo,
                                      skip_group_check=True)
                    if last and m < KD - 1:
                        t.then_inc(summed, 1)
                t.then_inc(multiplied[s], 1)

            for r in range(len(ranges)):
                u0 = r * (KF // 2)
                step(r, 0, u0, True, False)
                step(r, 1, u0, False, False)
                with pe.Fori(1, KF // 2 - 1) as it:
                    step(r, 0, it + u0, False, False)
                    step(r, 1, it + u0, False, False)
                step(r, 0, u0 + KF // 2 - 1, False, False)
                step(r, 1, u0 + KF // 2 - 1, False, True)

        @block.vector
        def _(dve):
            def add(r):
                t0, t1 = ranges[r]
                v = 1 if t1 <= CTX else 0
                dve.wait_ge(x_in, 16 * (r + 1))
                for m in range(KD):
                    if m < KD - 1:
                        dve.wait_ge(summed, (KD - 1) * r + m + 1)
                    else:
                        dve.wait_ge(multiplied[1], KF // 2 * (r + 1))
                    gate = G.MOD[:, layer, 5 * KD + m:5 * KD + m + 1, v]
                    xm = x[:, r % 2, m, 0:t1 - t0]
                    dve.scalar_tensor_tensor(out=xm, in0=acc[:, m, 0:t1 - t0], scalar=gate, in1=xm,
                                             op0=ALU.mult, op1=ALU.add).then_inc(added, 1)

            used = [0, 0]
            for r, (t0, t1) in enumerate(ranges):
                T = t1 - t0
                for i, its in enumerate(sweep(dve, KF, used, lag=True)):
                    for k, s, u, it, other in its:
                        dve.wait_ge(multiplied[s], u)
                        dve.wait_ge(w_hi_ready[s], u + 1)
                        dve.tensor_tensor(w_lo[:, s, 512:D], w_raw[:, s, 512:D], w_hi[:, s, 512:D].bitcast(F32),
                                          ALU.subtract).then_inc(w2_lo_ready[s], 1)
                        dve.wait_ge(h_hi_ready[s], u + 1)
                        dve.tensor_tensor(h_lo[:, s, 0:T], h_raw[:, s, 0:T], h_hi[:, s, 0:T].bitcast(F32),
                                          ALU.subtract).then_inc(h_lo_ready[s], 1)
                        if r >= 1 and i == 0 and s == 0:
                            add(r - 1)
            add(len(ranges) - 1)


class Tile:

    def __init__(self, q0, keys, kind=None):
        self.q0, self.kind = q0, kind
        self.pieces, self.kts, col = [], [], 0
        for a, n in keys:
            self.pieces.append((col, a, n))
            for o in range(0, n, P):
                self.kts.append((col + o, (a + o) // P, min(P, n - o)))
            col += n
        self.cols = col

    def score_parts(self, base):
        for col, tok, n in self.pieces:
            while n:
                m = min(n, 512 - (base + col) % 512)
                yield col, tok, m
                col, tok, n = col + m, tok + m, n - m


def attention(nc, G, name, mode, tiles, groups, q_src, k_src, v_src, q_toks, out, out_toks, IN=None):
    UNITS = 4
    mla, diff, swa, na = mode == "mla", mode == "diff", mode == "swa", mode == "na"
    rows = C_DQK if mla else P
    tq0, tq1 = q_toks
    TQ = tq1 - tq0
    nraw = 2 if mla else 1
    nw = 1 if diff else 2
    gs = max(len(g) for g in groups)
    kmax = max(len(t.kts) for t in tiles)
    smax = max(t.cols for t in tiles)
    NTL = len(tiles)
    N = UNITS * NTL
    group_of = {i: (g, p) for g, gr in enumerate(groups) for p, i in enumerate(gr)}
    with Stage(nc, name) as st:
        q_raw, k_raw, v_raw = st.sb("q_raw", [P, nraw, TQ]), st.sb("k_raw", [P, nraw, NT]), st.sb("v_raw", [P, NT])
        kpar = 1 if swa else 2
        if mla:
            QA, QB = st.sb("QH", [P, 2, 2, TQ], F32R), st.sb("QL", [P, 2, 2, TQ], F32R)
        else:
            QA = st.sb("QS", [P, 2, 2, TQ], F32R)
        KA, KB = st.sb("KA", [P, kpar, 2, NT], F32R), st.sb("KB", [P, kpar, 2, NT], F32R)
        V = st.sb("V", [P, kpar, NT // P, P])
        npr = 3
        PR = st.sb("PR", [P, npr, 2, smax])
        PT = st.sb("PT", [P, nw, kmax, 2 * gs * P])
        if nw == 2:
            diag = st.sb("diag", [P, 2, 2, P])
        opar = 2
        ob = st.sb("ob", [P, opar, NTL * P])
        stat = st.sb("stat", [P, 2, 8])
        if na:
            bias = st.sb("bias", [P, 2, 2, 5, CTX + NA_KEYS])
        if swa:
            mask = st.sb("mask", [P, 3, CTX + 3 * P])
        sw = 1536 if smax > 1024 else 1024
        NB = 8 - 2 * sw // 512
        sc = st.ps("sc", [P, 2, sw])
        tb = st.ps("tb", [P, NB, 512])
        q_in, k_in, v_in = st.sem("q_in"), st.sem("k_in"), st.sem("v_in")
        first_hi, first_lo, split = st.sem("first_hi"), st.sems("first_lo"), st.sem("split")
        mask_in, bias_in, bias_zero = st.sem("mask_in"), st.sems("bias_in"), st.sem("bias_zero")
        scored, maxed, exped, weighted = st.sems("scored"), st.sems("maxed"), st.sems("exped"), st.sems("weighted")
        t_ready, t_free = st.sems("t_ready", NB), st.sems("t_free", NB)
        chain, sink_exp, inverted = st.sem("chain"), st.sem("sink_exp"), st.sem("inverted")
        stored = st.sem("stored")
        block = st.block()

        def hi_parts(u, e):
            kp = 0 if swa else u % 2
            if mla:
                return [(QA[0:rows, u % 2, e, :], q_raw[0:rows, e, :]), (KA[0:rows, kp, e, :], k_raw[0:rows, e, :])]
            own, oth = slice(e * 64, e * 64 + 64), slice(64 - e * 64, P - e * 64)
            parts = [(QA[own, u % 2, e, :], q_raw[own, 0, :])]
            if not swa or u == 0:
                parts += [(KA[own, kp, e, :], k_raw[own, 0, :]), (KA[oth, kp, e, :], k_raw[own, 0, :])]
            return parts

        def lo_parts(u, e):
            kp = 0 if swa else u % 2
            if mla:
                return [(QB[0:rows, u % 2, e, :], q_raw[0:rows, e, :], QA[0:rows, u % 2, e, :]),
                        (KB[0:rows, kp, e, :], k_raw[0:rows, e, :], KA[0:rows, kp, e, :])]
            own, oth = slice(e * 64, e * 64 + 64), slice(64 - e * 64, P - e * 64)
            parts = [(QA[oth, u % 2, e, :], q_raw[own, 0, :], QA[own, u % 2, e, :])]
            if not swa or u == 0:
                parts += [(KB[x, kp, e, :], k_raw[own, 0, :], KA[own, kp, e, :]) for x in (own, oth)]
            return parts

        n_first = len(hi_parts(0, 0))
        n_unit = 4 * len(hi_parts(1, 0))

        def wait_split(eng, u, e):
            if u == 0:
                eng.wait_ge(first_hi, n_first * (e + 1))
                eng.wait_ge(first_lo[e], n_first)
            else:
                eng.wait_ge(split, n_unit * (u - 1) + n_unit // 2 * (e + 1))

        def bank_jobs(n):
            before, after = [], []
            if 2 <= n < N + 2:
                kts = tiles[(n - 2) % NTL].kts
                for e in range(nw):
                    full = [k for k in range(len(kts)) if kts[k][2] == P]
                    jobs = [("p", n - 2, e, full[c:c + 4]) for c in range(0, len(full), 4)]
                    jobs += [("p", n - 2, e, [k]) for k in range(len(kts)) if kts[k][2] < P]
                    if e == 0:
                        before, after = (jobs[:2], jobs[2:]) if diff else (jobs, [])
                    else:
                        after = after + jobs
            if n >= 3 and group_of[(n - 3) % NTL][1] == len(groups[group_of[(n - 3) % NTL][0]]) - 1:
                after.insert(0, ("o", group_no(n - 3), 0, 0))
            if n == 0:
                after += [("v", 0, 0, c) for c in range(3)]
            elif not swa and n % NTL == 5 and n // NTL + 1 < UNITS:
                after += [("v", n // NTL + 1, 0, c) for c in range(3)]
            return before, after

        def early(n, half):
            if n >= N:
                return 0
            return min(len(bank_jobs(n)[half]), len(list(tiles[n % NTL].score_parts(0))) - 1, 2 if mla and half == 0 else 0)

        def group_no(m):
            u, i = divmod(m, NTL)
            return u * len(groups) + group_of[i][0]

        number, uses = {}, 0
        for n in range(N + 3):
            for kind, a, e, c in bank_jobs(n)[0] + bank_jobs(n)[1]:
                number[kind, a, e] = uses
                uses += 1

        def wait_ready(eng, kind, a, e=0):
            eng.wait_ge(t_ready[number[kind, a, e] % NB], number[kind, a, e] // NB + 1)

        def wait_freed(eng, kind, a, e=0):
            eng.wait_ge(t_free[number[kind, a, e] % NB], number[kind, a, e] // NB + 1)

        def pt_cols(m):
            u, i = divmod(m, NTL)
            p = group_no(m) % 2 * gs + group_of[i][1]
            return p * P, (p + 1) * P

        @block.sync
        def _(sp):
            if swa:
                sp.dma_start(mask[:, :, :], IN["k_swa_mask"]).then_inc(mask_in, 16)

            def store(u):
                for g in range(len(groups)):
                    wait_freed(sp, "o", u * len(groups) + g)
                sp.dma_start(out[u * P:(u + 1) * P, out_toks[0]:out_toks[1]], ob[:, u % opar, :]).then_inc(stored, 16)

            for u in range(UNITS):
                if u >= 1:
                    for e in range(2):
                        wait_split(sp, u - 1, e)
                for r in range(nraw):
                    sp.dma_start(q_raw[0:rows, r, :], q_src(u, r)[:, tq0:tq1]).then_inc(q_in, 16)
                    if not swa or u == 0:
                        sp.dma_start(k_raw[0:rows, r, :], k_src(u, r)).then_inc(k_in, 16)
                if not swa or u == 0:
                    if u >= 1:
                        wait_ready(sp, "v", u - 1, 0)
                    sp.dma_start(v_raw[:, :], v_src(u)).then_inc(v_in, 16)
                if na:
                    if u >= 2:
                        sp.wait_ge(maxed[0], NTL * (u - 1))
                        sp.wait_ge(maxed[1], NTL * (u - 1))
                    for e in range(2):
                        for kind in range(5):
                            for rr in range(2):
                                skip = rr if NA_ROWS[kind] == 9 else 0
                                d0 = NA_D0[kind] - rr + skip
                                src = G.RPB[2 * u + e, d0:d0 + NA_H, :, :].rearrange("d c k -> c d k")
                                c0 = CTX + skip * GRID_W
                                dst = bias[rr * 64:rr * 64 + 64, u % 2, e, kind, c0:c0 + NA_H * GRID_W]
                                sp.dma_start(dst.rearrange("p (d k) -> p d k", k=64), src).then_inc(bias_in[u % 2], 16)
                if u >= 1:
                    store(u - 1)
            store(UNITS - 1)
            sp.wait_ge(stored, 16 * UNITS)

        @block.gpsimd
        def _(pool):
            if na:
                pool.memset(bias[:, :, :, :, 0:CTX], 0.0).then_inc(bias_zero, 1)
                for rr in range(2):
                    c0 = CTX + (0 if rr else NA_H * GRID_W)
                    pool.wait_ge(bias_zero, rr + 1)
                    pool.memset(bias[rr * 64:rr * 64 + 64, :, :, 2, c0:c0 + GRID_W], NEG).then_inc(bias_zero, 1)
            pool.wait_ge(first_hi, 2 * n_first)
            for dst, raw, high in lo_parts(0, 1):
                pool.tensor_tensor(dst, raw, high.bitcast(F32), ALU.subtract).then_inc(first_lo[1], 1)
            for u in range(1, UNITS):
                pool.wait_ge(q_in, 16 * nraw * (u + 1))
                if not swa:
                    pool.wait_ge(k_in, 16 * nraw * (u + 1))
                if u >= 2:
                    for e in range(2):
                        pool.wait_ge(scored[e], NTL * (u - 1))
                for e in range(2):
                    for dst, raw in hi_parts(u, e):
                        pool.tensor_copy(dst, raw).then_inc(split, 1)
                    pool.wait_ge(split, n_unit * (u - 1) + n_unit // 4 * (2 * e + 1))
                    for dst, raw, high in lo_parts(u, e):
                        pool.tensor_tensor(dst, raw, high.bitcast(F32), ALU.subtract).then_inc(split, 1)

        @block.tensor
        def _(pe):
            job = [0]

            def scores(n, e, jobs):
                u, i = divmod(n, NTL)
                t = tiles[i]
                ku, ke = (0, u // 2) if swa else (u % 2, e)
                wait_split(pe, u, e)
                if swa:
                    wait_split(pe, 0, ke)
                if n:
                    pe.wait_ge(maxed[e] if tiles[(n - 1) % NTL].kind is not None else exped[e], n)
                q = slice(t.q0 - tq0, t.q0 - tq0 + P)
                for x, (col, tok, m) in enumerate(t.score_parts(0)):
                    if 1 <= x <= len(jobs):
                        turn(jobs[x - 1:x])
                    o = sc[:, e, col:col + m]
                    if mla:
                        work = [(QA, KA), (QA, KB), (QB, KA)]
                    else:
                        work = [(QA, KA), (QA, KB)]
                    for j, (a, b) in enumerate(work):
                        last = pe.matmul(o, a[0:rows, u % 2, e, q], b[0:rows, ku, ke, tok:tok + m], start=j == 0,
                                         stop=j == len(work) - 1)
                last.then_inc(scored[e], 1)

            def turn(jobs):
                for kind, a, e, c in jobs:
                    bank, use = job[0] % NB, job[0] // NB
                    pe.wait_ge(t_free[bank], use)
                    if kind == "o":
                        values(a, bank)
                    elif kind == "v":
                        pe.wait_ge(v_in, 16 * (a + 1))
                        for k in range(4 * c, min(4 * c + 4, NT // P)):
                            last = pe.transpose(tb[:, bank, (k % 4) * P:(k % 4 + 1) * P], v_raw[:, k * P:(k + 1) * P],
                                                G.IDENT[:, :])
                        last.then_inc(t_ready[bank], 1)
                    else:
                        pe.wait_ge(weighted[e], a + 1)
                        t = tiles[a % NTL]
                        for x, k in enumerate(c):
                            col, _, ln = t.kts[k]
                            w = PR[:, a % npr, e, col:col + ln]
                            o = tb[0:ln, bank, x * P:(x + 1) * P]
                            if diff:
                                last = pe.transpose(o, w, G.IDENT[:, :])
                            else:
                                last = pe.matmul(o, w, diag[:, a % 2, e, :], start=True, stop=True)
                        last.then_inc(t_ready[bank], 1)
                    job[0] += 1

            def values(gn, bank):
                u, g = divmod(gn, len(groups))
                members = groups[g]
                m = u * NTL + members[-1]
                for x in range(u * NTL + members[0], m + 1):
                    for e in range(nw):
                        for bk in range(NB):
                            done = max([0] + [k // NB + 1 for k in tile_uses[x] if k % NB == bk])
                            if done:
                                pe.wait_ge(t_free[bk], done)
                c0 = pt_cols(u * NTL + members[0])[0]
                c1 = c0 + len(members) * P
                t = tiles[members[0]]
                for e in range(nw):
                    h = slice(0, P) if diff else slice(e * 64, e * 64 + 64)
                    vc = slice(u // 2 * 64, u // 2 * 64 + 64) if swa else h
                    for k, (_, vt, ln) in enumerate(t.kts):
                        last = pe.matmul(tb[h, bank, 0:c1 - c0], V[0:ln, 0 if swa else u % 2, vt, vc], PT[0:ln, e, k, c0:c1],
                                         start=k == 0, stop=k == len(t.kts) - 1)
                last.then_inc(t_ready[bank], 1)

            tile_uses, number_ = {}, 0
            for n in range(N + 3):
                for kind, a, e, c in bank_jobs(n)[0] + bank_jobs(n)[1]:
                    if kind == "p":
                        tile_uses.setdefault(a, []).append(number_)
                    number_ += 1
            for n in range(N + 3):
                for half in range(2):
                    jobs = bank_jobs(n)[half]
                    if n < N:
                        scores(n, half, jobs[:early(n, half)])
                    turn(jobs[early(n, half):])

        def evacuate(eng, copy, jobs, job):
            for what, a, e, c in jobs:
                bank, use = job[0] % NB, job[0] // NB
                job[0] += 1
                if bank % 2 != (0 if copy == "act" else 1):
                    continue
                eng.wait_ge(t_ready[bank], use + 1)
                if what == "v":
                    ks = range(4 * c, min(4 * c + 4, NT // P))
                    if a >= 2:
                        wait_ready(eng, "o", len(groups) * (a - 1) - 1)
                    dst = V[:, 0 if swa else a % 2, ks[0]:ks[-1] + 1, :]
                    src = tb[:, bank, 0:len(ks) * P].rearrange("p (k c) -> p k c", c=P)
                elif what == "o":
                    u, g = divmod(a, len(groups))
                    if u >= opar:
                        eng.wait_ge(stored, 16 * (u - opar + 1))
                    dst = ob[:, u % opar, groups[g][0] * P:(groups[g][-1] + 1) * P]
                    src = tb[:, bank, 0:len(groups[g]) * P]
                else:
                    ln = tiles[a % NTL].kts[c[0]][2]
                    before = group_no(a) - 2
                    if before >= 0:
                        wait_ready(eng, "o", before)
                    c0, c1 = pt_cols(a)
                    dst = PT[0:ln, e, c[0]:c[-1] + 1, c0:c1]
                    src = tb[0:ln, bank, 0:len(c) * P].rearrange("p (k c) -> p k c", c=P)
                if copy == "act":
                    eng.activation(dst, src, ACT.Copy).then_inc(t_free[bank], 1)
                else:
                    eng.tensor_copy(dst, src).then_inc(t_free[bank], 1)

        @block.scalar
        def _(act):
            job = [0]

            act.wait_ge(q_in, 16 * nraw)
            act.wait_ge(k_in, 16 * nraw)
            for e in range(2):
                for dst, raw in hi_parts(0, e):
                    act.activation(dst, raw, ACT.Copy).then_inc(first_hi, 1)
            for n in range(N + 3):
                if diff and 1 <= n <= N:
                    m = n - 1
                    w = PR[:, m % npr, 1, 0:tiles[m % NTL].cols]
                    act.wait_ge(inverted, m + 1)
                    act.activation(w, w, ACT.Copy, scale=stat[:, m % 2, 3:4]).then_inc(weighted[1], 1)
                for e in range(2):
                    evacuate(act, "act", bank_jobs(n)[e][:early(n, e)], job)
                    if n < N:
                        t = tiles[n % NTL]
                        act.wait_ge(maxed[e], n + 1)
                        if n >= npr and nw > e:
                            wait_ready(act, "p", n - npr, e)
                        elif n >= npr:
                            act.wait_ge(weighted[0], n - npr + 1)
                        src = PR[:, n % npr, e, 0:t.cols] if t.kind is not None else sc[:, e, 0:t.cols]
                        act.activation(PR[:, n % npr, e, 0:t.cols], src, ACT.Exp, bias=stat[:, n % 2, e:e + 1],
                                       accum_out=stat[:, n % 2, 2 + e:3 + e]).then_inc(exped[e], 1)
                    if swa and e == 1 and n < N:
                        act.activation(stat[:, n % 2, 6:8], stat[:, n % 2, 4:6], ACT.Exp).then_inc(sink_exp, 1)
                    evacuate(act, "act", bank_jobs(n)[e][early(n, e):], job)

        @block.vector
        def _(dve):
            job = [0]
            links = [0]

            def link(ins):
                links[0] += 1
                ins.then_inc(chain, 1)
                dve.wait_ge(chain, links[0])

            def invert(m):
                p = m % 2
                for e in range(2):
                    dve.wait_ge(exped[e], m + 1)
                s = stat[:, p, 2:4]
                if swa:
                    dve.wait_ge(sink_exp, m + 1)
                    link(dve.tensor_tensor(s, s, stat[:, p, 6:8], ALU.add))
                link(dve.reciprocal(s, s))
                if not diff:
                    for e in range(2):
                        if m >= 2:
                            wait_ready(dve, "p", m - 2, e)
                        dve.tensor_scalar(diag[:, p, e, :], G.IDENT[:, :], stat[:, p, 2 + e:3 + e], None, ALU.mult)\
                            .then_inc(weighted[e], 1)
                    return
                link(dve.tensor_scalar(stat[:, p, 2:3], stat[:, p, 2:3], G.LINV[:, 0:1], None, ALU.mult))
                dve.tensor_scalar(stat[:, p, 3:4], stat[:, p, 3:4], G.NLAM[:, 0:1], None, ALU.mult).then_inc(inverted, 1)

            def weigh(m):
                p, pr, cols = m % 2, m % npr, tiles[m % NTL].cols
                dve.wait_ge(weighted[1], m + 1)
                w = PR[:, pr, 0, 0:cols]
                dve.scalar_tensor_tensor(out=w, in0=w, scalar=stat[:, p, 2:3], in1=PR[:, pr, 1, 0:cols],
                                         op0=ALU.mult, op1=ALU.add).then_inc(weighted[0], 1)

            def biased_max(n, e):
                u, i = divmod(n, NTL)
                t = tiles[i]
                if na:
                    dve.wait_ge(bias_in[u % 2], 20 * 16 * (u // 2 + 1))
                dve.wait_ge(scored[e], n + 1)
                if n >= 2:
                    dve.wait_ge(exped[e], n - 1)
                s = sc[:, e, 0:t.cols]
                mx = stat[:, n % 2, e:e + 1]
                if t.kind is None:
                    dve.tensor_reduce(mx, s, AX, ALU.max, negate=True).then_inc(maxed[e], 1)
                    return
                if n >= npr:
                    wait_ready(dve, "p", n - npr, e)
                tab = bias[:, u % 2, e, t.kind, 0:t.cols] if na else mask[:, t.kind, 0:t.cols]
                link(dve.tensor_tensor_reduce(PR[:, n % npr, e, 0:t.cols], s, tab, 1.0, -3e38, ALU.add, ALU.max, mx))
                if swa:
                    sink = G.SINK[:, 2 * u + e:2 * u + e + 1]
                    link(dve.tensor_tensor(mx, mx, sink, ALU.max))
                    if n >= 2:
                        dve.wait_ge(sink_exp, n - 1)
                    link(dve.tensor_tensor(stat[:, n % 2, 4 + e:5 + e], sink, mx, ALU.subtract))
                dve.tensor_scalar(mx, mx, -1.0, None, ALU.mult).then_inc(maxed[e], 1)

            dve.wait_ge(first_hi, n_first)
            for dst, raw, high in lo_parts(0, 0):
                dve.tensor_tensor(dst, raw, high.bitcast(F32), ALU.subtract).then_inc(first_lo[0], 1)
            if swa:
                dve.wait_ge(mask_in, 16)
            if na:
                dve.wait_ge(bias_zero, 3)
            for n in range(N + 3):
                if not swa and 1 <= n <= N:
                    invert(n - 1)
                for e in range(2):
                    evacuate(dve, "dve", bank_jobs(n)[e][:early(n, e)], job)
                    if n < N:
                        biased_max(n, e)
                    if swa and e == 0 and 1 <= n <= N:
                        invert(n - 1)
                    if diff and e == 1 and 1 <= n <= N:
                        weigh(n - 1)
                    evacuate(dve, "dve", bank_jobs(n)[e][early(n, e):], job)


def transpose_out(nc, G, out):
    with Stage(nc, "xout") as st:
        xt = st.sb("xt", [P, 2, KD, P])
        tok = st.sb("tok", [P, 2, D])
        tps = st.ps("tps", [P, 2, KD, P])
        load, turn, copy_a, copy_v, store = (st.sems(n) for n in ("load", "turn", "copy_a", "copy_v", "store"))
        block = st.block()
        O = out.rearrange("a (t p) d -> (a t) p d", p=P)
        XT = G.X.rearrange("(k p) t -> p k t", p=P)
        n = LAT // P

        @block.sync
        def _(sp):
            for its in sweep(sp, n, [0, 0]):
                for m, s, u, it, other in its:
                    sp.wait_ge(turn[s], u)
                    sp.dma_start(xt[:, s, :, :], XT[:, :, bass.ds(CTX + m * P, P)]).then_inc(load[s], 16)

        @block.tensor
        def _(pe):
            for its in sweep(pe, n, [0, 0]):
                for m, s, u, it, other in its:
                    pe.wait_ge(load[s], 16 * u + 16)
                    pe.wait_ge(copy_a[s], u)
                    pe.wait_ge(copy_v[s], u)
                    for k in range(KD):
                        t = pe.transpose(tps[:, s, k, :], xt[:, s, k, :], G.IDENT[:, :])
                    t.then_inc(turn[s], 1)

        @block.scalar
        def _(act):
            used = [0, 0]
            for its in sweep(act, n, used):
                for m, s, u, it, other in its:
                    act.wait_ge(turn[s], u + 1)
                    act.wait_ge(store[s], 16 * u)
                    act.activation(tok[:, s, 0:512], tps[:, s, 0:4, :].rearrange("p a b -> p (a b)"), ACT.Copy).then_inc(copy_a[s], 1)
                    act.wait_ge(copy_a[s], u + 1)
                    act.wait_ge(copy_v[s], u + 1)
                    act.dma_start(O[bass.ds(m, 1)].rearrange("a p d -> (a p) d"), tok[:, s, :]).then_inc(store[s], 16)
            for s in range(2):
                act.wait_ge(store[s], 16 * used[s])

        @block.vector
        def _(dve):
            for its in sweep(dve, n, [0, 0]):
                for m, s, u, it, other in its:
                    dve.wait_ge(turn[s], u + 1)
                    dve.wait_ge(store[s], 16 * u)
                    dve.tensor_copy(tok[:, s, 512:1024], tps[:, s, 4:8, :].rearrange("p a b -> p (a b)")).then_inc(copy_v[s], 1)


class Globals:
    pass


def trunk(nc, IN, out):
    G = Globals()
    Stage.cleared = []
    ctx = ExitStack()
    with ctx:
        def sb(name, shape, dt=F32):
            return ctx.enter_context(nc.sbuf_tensor(name, shape, dt))

        def dram(name, shape):
            return nc.dram_tensor(name, shape, F32, kind="Internal").ap()

        G.IDENT, G.BLK64, G.ONES = sb("IDENT", [P, P]), sb("BLK64", [P, P]), sb("ONES", [P, P])
        G.ROT, G.ROT96, G.ROTG = sb("ROT", [P, P]), sb("ROT96", [C_DQK, C_DQK]), sb("ROTG", [P, 6, P])
        G.LINV, G.EPSL = sb("LINV", [P, 1]), sb("EPSL", [P, 1])
        G.EPSC, G.NLAM, G.SINK, G.CVEC = sb("EPSC", [P, 1]), sb("NLAM", [P, 1]), sb("SINK", [P, 8]), sb("CVEC", [P, 16])
        G.GV, G.PRM = sb("GV", [P, GV_N]), sb("PRM", [P, PRM_N])
        G.MOD, G.GS = sb("MOD", [P, DEPTH, 6 * KD, 2]), sb("GS", [P, DEPTH, 2, KD, 2])
        G.X, G.Y, G.Z, G.H = dram("X", [D, NT]), dram("Y", [3072, NT]), dram("Z", [D, NT]), dram("H", [FFN, NT])
        G.RPB = dram("RPB", [8, HALF_ROWS, GRID_W, GRID_W])
        G.Q, G.K, G.VM = dram("Q", [C_HEADS * C_DQK, NT]), dram("K", [C_HEADS * C_DQK, NT]), dram("VM", [512, NT])
        G.Y1 = dram("Y1", [1440, NT])

        load_parameters(nc, G, IN)
        modulation(nc, G, IN)
        transpose_in(nc, G, IN)

        def modulated(layer, which, t0):
            rs = [(v, max(a, t0), b) for v, a, b in ((1, 0, CTX), (0, CTX, NT)) if b > t0]
            scale = lambda k: [(G.GS[:, layer, which, k, v:v + 1], a, b) for v, a, b in rs]
            shift = lambda k: [(G.MOD[:, layer, 3 * which * KD + k, v:v + 1], a, b) for v, a, b in rs]
            return dict(scale=scale, shift=shift)

        def gain(col, t0, limit=99):
            return lambda k: [(G.GV[:, col + (k if limit == 99 else 0):col + (k if limit == 99 else 0) + 1], t0, NT)] if k < limit else []

        def ffn(layer, t0):
            with Stage(nc, f"fa{layer}") as st:
                act_h, act_l = st.sb("act_h", [P, KD, NT - t0], F32R), st.sb("act_l", [P, KD, NT - t0], F32R)
                op = Operand(G, G.X, KD, t0, NT, act_h, act_l, **modulated(layer, 1, t0))
                ffn_up(nc, G, f"up{layer}", IN["ffn_up"][layer], act_h, act_l, t0, layer, (t0, NT), G.H, op=op)
            ranges = ([(0, CTX)] if t0 == 0 else []) + chunks(CTX, NT)
            ffn_down(nc, G, f"dn{layer}", IN["ffn_down"][layer], G.H, layer, ranges)

        with Stage(nc, "a0") as st:
            act_h, act_l = st.sb("act_h", [P, KD, NT], F32R), st.sb("act_l", [P, KD, NT], F32R)
            op = Operand(G, G.X, KD, 0, NT, act_h, act_l, **modulated(0, 0, 0))
            both = (0, NT)
            heads = dict(mw=P, toks=both, rows=P, own=P, ones=G.BLK64, width=64)
            at = lambda c0: (lambda m, s, it: c0 + m * P)
            segs = [dict(heads, tiles=4, col=at(0), row=0, rope=G.ROTG[:, 0, :], gain=GV_AQ),
                    dict(heads, tiles=4, col=at(512), row=512, rope=G.ROTG[:, 1, :], gain=GV_AK),
                    dict(heads, tiles=4, col=at(1536), row=1536, rope=None, gain=GV_BQ),
                    dict(heads, tiles=4, col=at(2048), row=2048, rope=None, gain=GV_BK)]
            project_heads(nc, G, "qk0", IN["ev_w_in"][0], KD, act_h, act_l, 0, segs, G.Y, (IN["k_cos"], IN["k_sin"]), op=op)
            vsegs = [dict(mw=P, toks=both, tiles=4, col=at(1024), row=1024),
                     dict(mw=P, toks=both, tiles=4, col=at(2560), row=2560)]
            project_store(nc, G, "v0", IN["ev_w_in"][0], KD, act_h, act_l, 0, vsegs, G.Y)
        whole = [(0, NT)]
        ctx_tiles = [Tile(q, [(0, CTX)]) for q in range(0, CTX, P)]
        lat_tiles = [Tile(q, whole) for q in range(CTX, NT, P)]
        nlat = LAT // P
        row = lambda src, r0: (lambda u, r=0: src[r0 + u * P:r0 + u * P + P])
        attention(nc, G, "da", "diff", ctx_tiles + lat_tiles, [[i] for i in range(2 + nlat)],
                  row(G.Y, 0), row(G.Y, 512), row(G.Y, 1024), (0, NT), G.Z[0:512], (0, NT))
        na_tiles = []
        for i in range(nlat):
            kind = NA_KIND[i]
            r0 = NA_D0[kind] + 2 * i - 7
            na_tiles.append(Tile(CTX + i * P, [(0, CTX), (CTX + r0 * GRID_W, NA_ROWS[kind] * GRID_W)], kind))
        attention(nc, G, "na", "na", ctx_tiles + na_tiles, [[i] for i in range(2 + nlat)],
                  row(G.Y, 1536), row(G.Y, 2048), row(G.Y, 2560), (0, NT), G.Z[512:1024], (0, NT), IN)
        with Stage(nc, "o0") as st:
            act_h, act_l = st.sb("act_h", [P, KD, NT], F32R), st.sb("act_l", [P, KD, NT], F32R)
            op = Operand(G, G.Z, KD, 0, NT, act_h, act_l, norm=False, sub_tiles=4, mean_over=P,
                    scale=gain(GV_SUB, 0, 4))
            project_residual(nc, G, "out0", IN["ev_w_out"][0], KD, act_h, act_l, 0, 0, (0, NT), 2, op=op)
        ffn(0, 0)

        with Stage(nc, "a1") as st:
            act_h, act_l = st.sb("act_h", [P, KD, NT], F32R), st.sb("act_l", [P, KD, NT], F32R)
            op = Operand(G, G.X, KD, 0, NT, act_h, act_l, **modulated(1, 0, 0))
            lat = (CTX, NT)
            heads = dict(mw=P, rows=P, own=P, ones=G.BLK64, width=64)
            segs = [dict(heads, toks=lat, tiles=4, col=at(ODD_DQ), row=ODD_DQ, rope=G.ROTG[:, 2, :], gain=GV_DQ),
                    dict(heads, toks=both, tiles=1, col=at(ODD_DK), row=ODD_DK, rope=G.ROTG[:, 3, :], gain=GV_DK)]
            project_heads(nc, G, "qk1", IN["od_w_in"][0], KD, act_h, act_l, 0, segs, G.Y1, (IN["k_cos"], IN["k_sin"]), op=op)
            ssegs = [dict(mw=P, toks=lat, tiles=3, col=at(ODD_CQ), row=ODD_CQ),
                     dict(mw=P, toks=both, tiles=2, col=at(ODD_CKV), row=ODD_CKV),
                     dict(mw=P, toks=both, tiles=1, col=at(ODD_DV), row=ODD_DV),
                     dict(mw=C_ROPE, toks=both, tiles=1, col=at(ODD_CKR), row=ODD_CKR)]
            project_store(nc, G, "s1", IN["od_w_in"][0], KD, act_h, act_l, 0, ssegs, G.Y1)
        t96 = (IN["k_cos96"], IN["k_sin96"])
        with Stage(nc, "a2") as st:
            act_h, act_l = st.sb("act_h", [P, 3, LAT], F32R), st.sb("act_l", [P, 3, LAT], F32R)
            op = Operand(G, G.Y1[0:Q_LORA], 3, CTX, NT, act_h, act_l, mean_over=Q_LORA, scale=gain(GV_CQA, CTX))
            segs = [dict(mw=C_DQK, toks=lat, tiles=8, col=lambda m, s, it: m * C_DQK, row=0, rows=C_DQK, own=C_DQK,
                         ones=G.ONES, width=C_DQK, rope=G.ROTG[0:C_DQK, 4, :], gain=GV_CQ)]
            project_heads(nc, G, "mq", IN["c_w_qb"][0], 3, act_h, act_l, CTX, segs, G.Q, t96, op=op)
        with Stage(nc, "a3") as st:
            act_h, act_l = st.sb("act_h", [P, 2, NT], F32R), st.sb("act_l", [P, 2, NT], F32R)
            op = Operand(G, G.Y1[ODD_CKV:ODD_CKR], 2, 0, NT, act_h, act_l, mean_over=KV_LORA, scale=gain(GV_CKVA, 0))
            segs = [dict(mw=P, toks=both, tiles=8, col=at(0), row=0, rows=C_DQK, own=64,
                         ones=G.ONES, width=C_DQK, rope=G.ROTG[0:C_DQK, 5, :], gain=GV_CK)]
            project_heads(nc, G, "mk", IN["c_w_kvb"][0], 2, act_h, act_l, 0, segs, G.K, t96,
                          kr=G.Y1[ODD_CKR:ODD_DQ], v_out=G.VM, op=op)
        head = lambda src: (lambda u, r: src[(2 * u + r) * C_DQK:(2 * u + r + 1) * C_DQK])
        attention(nc, G, "ma", "mla", lat_tiles, [[i, i + 1] for i in range(0, nlat, 2)], head(G.Q), head(G.K), row(G.VM, 0),
                  lat, G.Z[0:512], lat)
        swa_tiles = []
        for i in range(nlat):
            a, b = max(0, (i - 1) * P), min(LAT, (i + 2) * P)
            swa_tiles.append(Tile(CTX + i * P, [(0, CTX), (CTX + a, b - a)], 0 if i == 0 else 2 if i == nlat - 1 else 1))
        one = lambda r0: (lambda u, r=0: G.Y1[r0:r0 + P])
        attention(nc, G, "sw", "swa", swa_tiles, [[i] for i in range(nlat)], row(G.Y1, ODD_DQ), one(ODD_DK), one(ODD_DV),
                  lat, G.Z[512:1024], lat, IN)
        with Stage(nc, "o1") as st:
            act_h, act_l = st.sb("act_h", [P, KD, LAT], F32R), st.sb("act_l", [P, KD, LAT], F32R)
            op = Operand(G, G.Z, KD, CTX, NT, act_h, act_l, norm=False)
            project_residual(nc, G, "out1", IN["od_w_out"][0], KD, act_h, act_l, CTX, 1, lat, 2, op=op)
        ffn(1, CTX)
        transpose_out(nc, G, out)


def shape_constants():
    f = np.float32
    k = {"k_ident": np.eye(P, dtype=f)}
    blk = np.zeros((P, P), f)
    rot = np.zeros((P, P), f)
    for h in (0, 64):
        blk[h:h + 64, h:h + 64] = 1
        for i in range(32):
            rot[h + 32 + i, h + i] = -1
            rot[h + i, h + 32 + i] = 1
    rot96 = np.zeros((C_DQK, C_DQK), f)
    for i in range(C_ROPE // 2):
        rot96[80 + i, 64 + i] = -1
        rot96[64 + i, 80 + i] = 1
    k["k_blk64"], k["k_rot"], k["k_rot96"] = blk, rot, rot96

    def angles(dim):
        t = np.arange(LAT)
        quarter = dim // 4
        inv = (f(10000.0) ** (-np.arange(quarter, dtype=f) / f(quarter))).astype(f)
        ang = np.concatenate([(t // GRID_W).astype(f)[:, None] * inv, (t % GRID_W).astype(f)[:, None] * inv], -1)
        return np.cos(ang).T.astype(f), np.sin(ang).T.astype(f)

    c, s = angles(64)
    cos, sin = np.ones((P, NT), f), np.zeros((P, NT), f)
    for r in range(0, P, 32):
        cos[r:r + 32, CTX:], sin[r:r + 32, CTX:] = c, s
    c, s = angles(C_ROPE)
    cos96, sin96 = np.ones((C_DQK, NT), f), np.zeros((C_DQK, NT), f)
    for r in (64, 80):
        cos96[r:r + 16, CTX:], sin96[r:r + 16, CTX:] = c, s
    k["k_cos"], k["k_sin"], k["k_cos96"], k["k_sin96"] = cos, sin, cos96, sin96

    q, j = np.arange(P)[:, None], np.arange(3 * P)[None, :]
    band = np.where(np.abs(j - P - q) <= P, f(0), f(NEG))
    swa = np.zeros((P, 3, CTX + 3 * P), f)
    swa[:, 0, CTX:CTX + 2 * P] = band[:, P:]
    swa[:, 1, CTX:] = band
    swa[:, 2, CTX:CTX + 2 * P] = band[:, :2 * P]
    k["k_swa_mask"] = swa
    return k


INPUTS = ["x", "c", "ctx", "c_ctx", "ada_w", "ada_b", "norm_mix", "norm_ffn", "ffn_up", "ffn_conv_w", "ffn_conv_b",
          "ffn_down", "ev_w_in", "ev_w_out", "a_q_norm", "a_k_norm", "a_lam_q1", "a_lam_k1", "a_lam_q2", "a_lam_k2",
          "a_subln", "b_q_norm", "b_k_norm", "b_rpb", "od_w_in", "od_w_out", "c_q_a_norm", "c_w_qb", "c_kv_a_norm",
          "c_w_kvb", "c_q_norm", "c_k_norm", "d_q_norm", "d_k_norm", "d_sink"]


def kernel(**inputs):
    import concourse.bacc as bacc
    from concourse.bass_utils import run_bass_kernel_spmd

    nc = bacc.Bacc("TRN2", target_bir_lowering=False, num_devices=1)
    arrays, args = {}, {}
    for name, a in [(n, inputs[n]) for n in INPUTS] + list(shape_constants().items()):
        a = np.ascontiguousarray(a)
        arrays[f"in_{name}"] = a
        args[name] = nc.dram_tensor(f"in_{name}", a.shape, mybir.dt.from_np(a.dtype), kind="ExternalInput").ap()
    out = nc.dram_tensor("out", (1, LAT, D), F32, kind="ExternalOutput").ap()
    trunk(nc, args, out)
    r = run_bass_kernel_spmd(nc, [arrays], core_ids=[0])
    return r.results[0]["out"]
```
